# Optimizing a Trainium2 kernel written in Bass

```python
import jax, jax.numpy as jnp
from jax import lax
import numpy as np

D_MODEL = 1024
BATCH = 1
SEQ = 512
DEPTH = 1

HEAD_DIM = 64
ATTN_HEADS = 8
ATTN_W = ATTN_HEADS * HEAD_DIM
CONV_W = 256
MEM_HEADS = 4
MEM_W = MEM_HEADS * HEAD_DIM
MIX_W = ATTN_W + CONV_W + MEM_W
N_MEM = 256
DILATED_PATTERNS = ((128, 1), (512, 4), (2048, 16))
ROPE_THETA = 500000.0
ROT_DIM = HEAD_DIM // 4
CONV_K = 31
FFN_CONV_K = 3
D_FF = 2816
IN_COLS = 3 * ATTN_W + 2 * CONV_W + MEM_W
SPLITS = (ATTN_W, 2 * ATTN_W, 3 * ATTN_W, 3 * ATTN_W + 2 * CONV_W)
NORM_EPS = 1e-6
NEG_INF = -1e30


def rms_norm(x, g):
    xf = x.astype(jnp.float32)
    y = xf * lax.rsqrt(jnp.mean(xf * xf, axis=-1, keepdims=True) + NORM_EPS)
    return (y * g.astype(jnp.float32)).astype(x.dtype)

def layer_norm(x, g, b):
    xf = x.astype(jnp.float32)
    mu = jnp.mean(xf, axis=-1, keepdims=True)
    var = jnp.mean(jnp.square(xf - mu), axis=-1, keepdims=True)
    y = (xf - mu) * lax.rsqrt(var + NORM_EPS)
    return (y * g.astype(jnp.float32) + b.astype(jnp.float32)).astype(x.dtype)

def partial_rotary(x, positions):
    inv_freq = ROPE_THETA ** (-jnp.arange(0, ROT_DIM, 2, dtype=jnp.float32) / ROT_DIM)
    ang = positions.astype(jnp.float32)[..., None] * inv_freq
    cos = jnp.cos(ang)[:, :, None, :]
    sin = jnp.sin(ang)[:, :, None, :]
    xr = x[..., :ROT_DIM].astype(jnp.float32)
    x1, x2 = xr[..., : ROT_DIM // 2], xr[..., ROT_DIM // 2:]
    rot = jnp.concatenate([x1 * cos - x2 * sin, x2 * cos + x1 * sin], axis=-1)
    return jnp.concatenate([rot.astype(x.dtype), x[..., ROT_DIM:]], axis=-1)

def depthwise_conv(x, w, b):
    k = w.shape[0]
    y = lax.conv_general_dilated(
        x, w[:, None, :].astype(x.dtype), window_strides=(1,),
        padding=[(k // 2, k // 2)], dimension_numbers=("NWC", "WIO", "NWC"),
        feature_group_count=x.shape[-1])
    return y + b.astype(x.dtype)

def banded_attention(q, k, v, half):
    n, L, H, Dh = q.shape
    blk = half
    nb = -(-L // blk)
    Lp = nb * blk
    qb = jnp.pad(q, ((0, 0), (0, Lp - L), (0, 0), (0, 0))).reshape(n, nb, blk, H, Dh)

    def halo(t):
        tp = jnp.pad(t, ((0, 0), (blk, Lp - L + blk), (0, 0), (0, 0))).reshape(n, nb + 2, blk, H, Dh)
        return jnp.concatenate([tp[:, :-2], tp[:, 1:-1], tp[:, 2:]], axis=2)

    kb, vb = halo(k), halo(v)
    s = jnp.einsum("nbqhd,nbkhd->nbhqk", qb, kb).astype(jnp.float32) * (Dh ** -0.5)
    bidx = jnp.arange(nb)[:, None, None]
    qi = jnp.arange(blk)[None, :, None]
    kj = jnp.arange(3 * blk)[None, None, :]
    key_pos = bidx * blk - blk + kj
    valid = (jnp.abs(kj - blk - qi) <= half) & (key_pos >= 0) & (key_pos < L)
    s = jnp.where(valid[None, :, None], s, NEG_INF)
    m = jnp.max(s, axis=-1, keepdims=True)
    p = jnp.exp(s - m)
    den = jnp.sum(p, axis=-1, keepdims=True)
    o = jnp.einsum("nbhqk,nbkhd->nbqhd", p, vb.astype(jnp.float32))
    o = o / jnp.transpose(den, (0, 1, 3, 2, 4))
    lse = jnp.transpose((m + jnp.log(den))[..., 0], (0, 1, 3, 2))
    return o.reshape(n, Lp, H, Dh)[:, :L], lse.reshape(n, Lp, H)[:, :L]

def dilated_attention(q, k, v, window, dil):
    B, S, H, Dh = q.shape
    L = S // dil

    def to_sub(t):
        return t.reshape(B, L, dil, H, Dh).transpose(0, 2, 1, 3, 4).reshape(B * dil, L, H, Dh)

    o, lse = banded_attention(to_sub(q), to_sub(k), to_sub(v), window // (2 * dil))
    o = o.reshape(B, dil, L, H, Dh).transpose(0, 2, 1, 3, 4).reshape(B, S, H, Dh)
    lse = lse.reshape(B, dil, L, H).transpose(0, 2, 1, 3).reshape(B, S, H)
    return o, lse

def first_inputs(seed: int = 0) -> dict:
    key = jax.random.key(seed)
    ks = jax.random.split(key, 24)
    f32 = jnp.float32

    def nrm(k, shape, scale):
        return jax.random.normal(k, shape, f32) * scale

    def gain(k, shape):
        return 1.0 + 0.02 * jax.random.normal(k, shape, f32)

    offsets = jax.random.randint(ks[2], (BATCH, 1), 0, 1024, dtype=jnp.int32)
    positions = (jnp.arange(SEQ, dtype=jnp.int32)[None, :] + offsets).astype(jnp.int32)
    return {
        "x": nrm(ks[0], (BATCH, SEQ, D_MODEL), 1.0),
        "mem": nrm(ks[1], (BATCH, N_MEM, D_MODEL), 1.0),
        "positions": positions,
        "mix_norm_g": gain(ks[3], (DEPTH, D_MODEL)),
        "mem_norm_g": gain(ks[4], (DEPTH, D_MODEL)),
        "w_in": nrm(ks[5], (DEPTH, D_MODEL, IN_COLS), D_MODEL ** -0.5),
        "w_mem_kv": nrm(ks[6], (DEPTH, D_MODEL, 2 * MEM_W), D_MODEL ** -0.5),
        "q_norm_g": gain(ks[7], (DEPTH, HEAD_DIM)),
        "k_norm_g": gain(ks[8], (DEPTH, HEAD_DIM)),
        "mq_norm_g": gain(ks[9], (DEPTH, HEAD_DIM)),
        "mk_norm_g": gain(ks[10], (DEPTH, HEAD_DIM)),
        "conv_dw_w": nrm(ks[11], (DEPTH, CONV_K, CONV_W), CONV_K ** -0.5),
        "conv_dw_b": nrm(ks[12], (DEPTH, CONV_W), 0.02),
        "conv_ln_g": gain(ks[13], (DEPTH, CONV_W)),
        "conv_ln_b": nrm(ks[14], (DEPTH, CONV_W), 0.02),
        "w_out": nrm(ks[15], (DEPTH, MIX_W, D_MODEL), MIX_W ** -0.5),
        "ffn_norm_g": gain(ks[16], (DEPTH, D_MODEL)),
        "w_up": nrm(ks[17], (DEPTH, D_MODEL, 2 * D_FF), D_MODEL ** -0.5),
        "ffn_dw_w": nrm(ks[18], (DEPTH, FFN_CONV_K, 2 * D_FF), FFN_CONV_K ** -0.5),
        "ffn_dw_b": nrm(ks[19], (DEPTH, 2 * D_FF), 0.02),
        "w_down": nrm(ks[20], (DEPTH, D_FF, D_MODEL), D_FF ** -0.5),
    }

def first_block(x, mem, positions, mix_norm_g, mem_norm_g, w_in, w_mem_kv, q_norm_g, k_norm_g,
              mq_norm_g, mk_norm_g, conv_dw_w, conv_dw_b, conv_ln_g, conv_ln_b, w_out,
              ffn_norm_g, w_up, ffn_dw_w, ffn_dw_b, w_down):
    B, S, _ = x.shape
    h = x
    for l in range(DEPTH):
        hn = rms_norm(h, mix_norm_g[l])
        proj = hn @ w_in[l]
        q, k, v, glu, qm = jnp.split(proj, SPLITS, axis=-1)

        q = partial_rotary(rms_norm(q.reshape(B, S, ATTN_HEADS, HEAD_DIM), q_norm_g[l]), positions)
        k = partial_rotary(rms_norm(k.reshape(B, S, ATTN_HEADS, HEAD_DIM), k_norm_g[l]), positions)
        v = v.reshape(B, S, ATTN_HEADS, HEAD_DIM)
        outs, lses = [], []
        for window, dil in DILATED_PATTERNS:
            o, lse = dilated_attention(q, k, v, window, dil)
            outs.append(o)
            lses.append(lse)
        wts = jax.nn.softmax(jnp.stack(lses, axis=0), axis=0)
        attn = jnp.sum(wts[..., None] * jnp.stack(outs, axis=0), axis=0)
        attn = attn.astype(h.dtype).reshape(B, S, ATTN_W)

        ga, gg = jnp.split(glu, 2, axis=-1)
        c = ga * jax.nn.sigmoid(gg)
        c = depthwise_conv(c, conv_dw_w[l], conv_dw_b[l])
        c = jax.nn.silu(layer_norm(c, conv_ln_g[l], conv_ln_b[l]))

        qm = rms_norm(qm.reshape(B, S, MEM_HEADS, HEAD_DIM), mq_norm_g[l])
        kvm = rms_norm(mem, mem_norm_g[l]) @ w_mem_kv[l]
        km, vm = jnp.split(kvm, 2, axis=-1)
        km = rms_norm(km.reshape(B, N_MEM, MEM_HEADS, HEAD_DIM), mk_norm_g[l])
        vm = vm.reshape(B, N_MEM, MEM_HEADS, HEAD_DIM)
        sm = jnp.einsum("bshd,bmhd->bhsm", qm, km).astype(jnp.float32) * (HEAD_DIM ** -0.5)
        pm = jax.nn.softmax(sm, axis=-1)
        mo = jnp.einsum("bhsm,bmhd->bshd", pm, vm.astype(jnp.float32))
        mo = mo.astype(h.dtype).reshape(B, S, MEM_W)

        mixed = jnp.concatenate([attn, c, mo], axis=-1)
        h = h + mixed @ w_out[l]

        f = rms_norm(h, ffn_norm_g[l]) @ w_up[l]
        f = depthwise_conv(f, ffn_dw_w[l], ffn_dw_b[l])
        fg, fu = jnp.split(f, 2, axis=-1)
        h = h + (jax.nn.silu(fg) * fu) @ w_down[l]
    return h


DEPTH_2 = 2

FOX_HEADS = 8
NSA_HEADS = 8
NSA_KV_HEADS = 2
NSA_GROUP = NSA_HEADS // NSA_KV_HEADS
CMP_BLOCK = 32
CMP_STRIDE = 16
CMP_HIDDEN = 4 * HEAD_DIM
SEL_BLOCK = 64
SEL_TOPK = 16
WINDOW = 512
Q_BLOCK = 128
ROPE_DIM = HEAD_DIM // 4
D_FF_2 = 4 * D_MODEL
RMS_EPS = 1e-6
FORGET_BIAS_INIT = 3.0
FORCE_SCORE = 1e6
NEG_BIG = -1e30

FOX_W = FOX_HEADS * HEAD_DIM
NSA_W = NSA_HEADS * HEAD_DIM
KV_W = NSA_KV_HEADS * HEAD_DIM
SPLITS_2 = (FOX_W, FOX_W, FOX_W, FOX_HEADS, NSA_W, 6 * KV_W, 3 * NSA_HEADS, D_MODEL, D_MODEL)
D_IN = sum(SPLITS_2)


def rmsnorm(x, g):
    xf = x.astype(jnp.float32)
    y = xf * lax.rsqrt(jnp.mean(xf * xf, axis=-1, keepdims=True) + RMS_EPS)
    return (y * g.astype(jnp.float32)).astype(x.dtype)

def partial_rope(t, pos):
    half = ROPE_DIM // 2
    inv = ROPE_THETA ** (-jnp.arange(half, dtype=jnp.float32) / half)
    ang = pos.astype(jnp.float32)[:, None] * inv[None, :]
    cos, sin = jnp.cos(ang), jnp.sin(ang)
    x1 = t[..., :half].astype(jnp.float32)
    x2 = t[..., half:ROPE_DIM].astype(jnp.float32)
    rot = jnp.concatenate([x1 * cos - x2 * sin, x2 * cos + x1 * sin], axis=-1)
    return jnp.concatenate([rot.astype(t.dtype), t[..., ROPE_DIM:]], axis=-1)

def to_heads(t, n):
    B, T, _ = t.shape
    return t.reshape(B, T, n, HEAD_DIM).transpose(0, 2, 1, 3)

def from_heads(o):
    B, H, T, dh = o.shape
    return o.transpose(0, 2, 1, 3).reshape(B, T, H * dh)

def n_cmp_blocks(T):
    return (T - CMP_BLOCK) // CMP_STRIDE + 1

def cmp_end_positions(T):
    return jnp.arange(n_cmp_blocks(T)) * CMP_STRIDE + CMP_BLOCK - 1

def cmp_to_sel_matrix(T):
    nc, n_sel = n_cmp_blocks(T), T // SEL_BLOCK
    cs = np.arange(nc) * CMP_STRIDE
    ce = cs + CMP_BLOCK
    ss = np.arange(n_sel) * SEL_BLOCK
    se = ss + SEL_BLOCK
    ov = np.clip(np.minimum(ce[:, None], se[None, :]) - np.maximum(cs[:, None], ss[None, :]), 0, None)
    return (ov / CMP_BLOCK).astype(np.float32)

def fox_attention(q, k, v, log_f):
    B, H, T, dh = q.shape
    c = jnp.cumsum(log_f, axis=-1)
    nb = T // Q_BLOCK
    qb = q.reshape(B, H, nb, Q_BLOCK, dh).transpose(2, 0, 1, 3, 4)
    cb = c.reshape(B, H, nb, Q_BLOCK).transpose(2, 0, 1, 3)
    kpos = jnp.arange(T)
    scale = HEAD_DIM ** -0.5

    def block(args):
        i, qi, ci = args
        qpos = i * Q_BLOCK + jnp.arange(Q_BLOCK)
        s = jnp.einsum('bhqd,bhkd->bhqk', qi, k, preferred_element_type=jnp.float32) * scale
        s = s + ci[..., :, None] - c[..., None, :]
        s = jnp.where(kpos[None, :] <= qpos[:, None], s, -jnp.inf)
        p = jax.nn.softmax(s, axis=-1)
        return jnp.einsum('bhqk,bhkd->bhqd', p.astype(v.dtype), v)

    out = lax.map(block, (jnp.arange(nb), qb, cb))
    return out.transpose(1, 2, 0, 3, 4).reshape(B, H, T, dh)

def compress_blocks(t, pos_emb, w1, b1, w2, b2):
    B, G, T, dh = t.shape
    nc = n_cmp_blocks(T)
    idx = np.arange(nc)[:, None] * CMP_STRIDE + np.arange(CMP_BLOCK)[None, :]
    blocks = t[:, :, idx, :] + pos_emb
    flat = blocks.reshape(B, G, nc, CMP_BLOCK * dh)
    return jax.nn.gelu(flat @ w1 + b1) @ w2 + b2

def nsa_attention(q, kc, vc, ks, vs, kw, vw):
    B, G, R, T, dh = q.shape
    n_sel = T // SEL_BLOCK
    top = min(SEL_TOPK, n_sel)
    nb = T // Q_BLOCK
    scale = HEAD_DIM ** -0.5
    cmp_end = cmp_end_positions(T)
    sel_map = jnp.asarray(cmp_to_sel_matrix(T))
    ks_blocks = ks.reshape(B, G, n_sel, SEL_BLOCK, dh)
    vs_blocks = vs.reshape(B, G, n_sel, SEL_BLOCK, dh)
    pad = ((0, 0), (0, 0), (WINDOW, 0), (0, 0))
    kw_pad = jnp.pad(kw, pad)
    vw_pad = jnp.pad(vw, pad)
    gather = jax.vmap(jax.vmap(lambda blocks, ix: blocks[ix]))
    qb = q.reshape(B, G, R, nb, Q_BLOCK, dh).transpose(3, 0, 1, 2, 4, 5)
    sel_ids = jnp.arange(n_sel)
    blk_start = sel_ids * SEL_BLOCK

    def block(args):
        i, qi = args
        q0 = i * Q_BLOCK
        qpos = q0 + jnp.arange(Q_BLOCK)
        s = jnp.einsum('bgrqd,bgnd->bgrqn', qi, kc, preferred_element_type=jnp.float32) * scale
        valid_c = cmp_end[None, :] <= qpos[:, None]
        p_c = jax.nn.softmax(jnp.where(valid_c, s, NEG_BIG), axis=-1) * valid_c
        o_c = jnp.einsum('bgrqn,bgnd->bgrqd', p_c.astype(vc.dtype), vc)
        imp = jnp.einsum('bgrqn,ns->bgqs', p_c, sel_map)
        future = blk_start[None, :] > qpos[:, None]
        forced = (sel_ids[None, :] == (qpos // SEL_BLOCK)[:, None]) | (sel_ids[None, :] == 0)
        imp = jnp.where(future, -1.0, jnp.where(forced, FORCE_SCORE, imp))
        _, idx = lax.top_k(imp, top)
        kg = gather(ks_blocks, idx).reshape(B, G, Q_BLOCK, top * SEL_BLOCK, dh)
        vg = gather(vs_blocks, idx).reshape(B, G, Q_BLOCK, top * SEL_BLOCK, dh)
        kpos = (idx[..., None] * SEL_BLOCK + jnp.arange(SEL_BLOCK)).reshape(B, G, Q_BLOCK, top * SEL_BLOCK)
        valid_s = kpos <= qpos[None, None, :, None]
        s = jnp.einsum('bgrqd,bgqkd->bgrqk', qi, kg, preferred_element_type=jnp.float32) * scale
        p_s = jax.nn.softmax(jnp.where(valid_s[:, :, None], s, -jnp.inf), axis=-1)
        o_s = jnp.einsum('bgrqk,bgqkd->bgrqd', p_s.astype(vg.dtype), vg)
        kwin = lax.dynamic_slice_in_dim(kw_pad, q0, WINDOW + Q_BLOCK, axis=2)
        vwin = lax.dynamic_slice_in_dim(vw_pad, q0, WINDOW + Q_BLOCK, axis=2)
        kpos_w = q0 - WINDOW + jnp.arange(WINDOW + Q_BLOCK)
        diff = qpos[:, None] - kpos_w[None, :]
        valid_w = (kpos_w[None, :] >= 0) & (diff >= 0) & (diff < WINDOW)
        s = jnp.einsum('bgrqd,bgkd->bgrqk', qi, kwin, preferred_element_type=jnp.float32) * scale
        p_w = jax.nn.softmax(jnp.where(valid_w, s, -jnp.inf), axis=-1)
        o_w = jnp.einsum('bgrqk,bgkd->bgrqd', p_w.astype(vwin.dtype), vwin)
        return o_c, o_s, o_w

    o_c, o_s, o_w = lax.map(block, (jnp.arange(nb), qb))
    unblock = lambda o: o.transpose(1, 2, 3, 0, 4, 5).reshape(B, G, R, T, dh)
    return unblock(o_c), unblock(o_s), unblock(o_w)

def hybrid_layer(x, norm_mix, w_in, b_forget, cmp_pos, cmp_w1, cmp_b1, cmp_w2, cmp_b2,
                 w_o_fox, w_o_nsa, w_out, norm_mlp, w_up, w_down):
    B, T, _ = x.shape
    h = rmsnorm(x, norm_mix)
    proj = h @ w_in
    q_a, k_a, v_a, f_a, q_b, kv_b, g_b, gate_a, gate_b = jnp.split(
        proj, np.cumsum(SPLITS_2)[:-1].tolist(), axis=-1)
    log_f = jax.nn.log_sigmoid((f_a + b_forget).astype(jnp.float32)).transpose(0, 2, 1)
    o_a = fox_attention(to_heads(q_a, FOX_HEADS), to_heads(k_a, FOX_HEADS), to_heads(v_a, FOX_HEADS), log_f)
    y_a = from_heads(o_a) @ w_o_fox
    pos = jnp.arange(T)
    q_n = partial_rope(to_heads(q_b, NSA_HEADS), pos).reshape(B, NSA_KV_HEADS, NSA_GROUP, T, HEAD_DIM)
    kc, vc, ks, vs, kw, vw = [to_heads(t, NSA_KV_HEADS) for t in jnp.split(kv_b, 6, axis=-1)]
    kc = compress_blocks(kc, cmp_pos[0], cmp_w1[0], cmp_b1[0], cmp_w2[0], cmp_b2[0])
    kc = partial_rope(kc, cmp_end_positions(T))
    vc = compress_blocks(vc, cmp_pos[1], cmp_w1[1], cmp_b1[1], cmp_w2[1], cmp_b2[1])
    ks = partial_rope(ks, pos)
    kw = partial_rope(kw, pos)
    o_c, o_s, o_w = nsa_attention(q_n, kc, vc, ks, vs, kw, vw)
    g = jax.nn.sigmoid(g_b).reshape(B, T, NSA_HEADS, 3).transpose(0, 2, 1, 3)
    g = g.reshape(B, NSA_KV_HEADS, NSA_GROUP, T, 3)
    o_n = g[..., 0:1] * o_c + g[..., 1:2] * o_s + g[..., 2:3] * o_w
    y_b = from_heads(o_n.reshape(B, NSA_HEADS, T, HEAD_DIM)) @ w_o_nsa
    mixed = jax.nn.sigmoid(gate_a) * y_a + jax.nn.sigmoid(gate_b) * y_b
    x = x + mixed @ w_out
    h = rmsnorm(x, norm_mlp)
    return x + jnp.square(jax.nn.relu(h @ w_up)) @ w_down

def second_inputs(seed: int = 0) -> dict:
    key = jax.random.key(seed)
    ks = jax.random.split(key, 17)
    f32 = jnp.float32
    nrm = lambda k, shape, fan_in: jax.random.normal(k, shape, f32) * fan_in ** -0.5
    return {
        'x': jax.random.normal(ks[0], (BATCH, SEQ, D_MODEL), f32),
        'norm_mix': 1.0 + 0.02 * jax.random.normal(ks[1], (DEPTH_2, D_MODEL), f32),
        'w_in': nrm(ks[2], (DEPTH_2, D_MODEL, D_IN), D_MODEL),
        'b_forget': FORGET_BIAS_INIT + 0.1 * jax.random.normal(ks[3], (DEPTH_2, FOX_HEADS), f32),
        'cmp_pos': 0.02 * jax.random.normal(ks[4], (DEPTH_2, 2, CMP_BLOCK, HEAD_DIM), f32),
        'cmp_w1': nrm(ks[5], (DEPTH_2, 2, CMP_BLOCK * HEAD_DIM, CMP_HIDDEN), CMP_BLOCK * HEAD_DIM),
        'cmp_b1': 0.02 * jax.random.normal(ks[6], (DEPTH_2, 2, CMP_HIDDEN), f32),
        'cmp_w2': nrm(ks[7], (DEPTH_2, 2, CMP_HIDDEN, HEAD_DIM), CMP_HIDDEN),
        'cmp_b2': 0.02 * jax.random.normal(ks[8], (DEPTH_2, 2, HEAD_DIM), f32),
        'w_o_fox': nrm(ks[9], (DEPTH_2, FOX_W, D_MODEL), FOX_W),
        'w_o_nsa': nrm(ks[10], (DEPTH_2, NSA_W, D_MODEL), NSA_W),
        'w_out': nrm(ks[11], (DEPTH_2, D_MODEL, D_MODEL), D_MODEL),
        'norm_mlp': 1.0 + 0.02 * jax.random.normal(ks[12], (DEPTH_2, D_MODEL), f32),
        'w_up': nrm(ks[13], (DEPTH_2, D_MODEL, D_FF_2), D_MODEL),
        'w_down': 0.5 * nrm(ks[14], (DEPTH_2, D_FF_2, D_MODEL), D_FF_2),
        'norm_final': 1.0 + 0.02 * jax.random.normal(ks[15], (D_MODEL,), f32),
    }

def second_block(x, norm_mix, w_in, b_forget, cmp_pos, cmp_w1, cmp_b1, cmp_w2, cmp_b2,
              w_o_fox, w_o_nsa, w_out, norm_mlp, w_up, w_down, norm_final):
    for l in range(DEPTH_2):
        x = hybrid_layer(x, norm_mix[l], w_in[l], b_forget[l], cmp_pos[l], cmp_w1[l], cmp_b1[l],
                         cmp_w2[l], cmp_b2[l], w_o_fox[l], w_o_nsa[l], w_out[l],
                         norm_mlp[l], w_up[l], w_down[l])
    return rmsnorm(x, norm_final)


def setup_inputs(seed=0):
    out = dict(first_inputs(seed))
    for name, value in second_inputs(seed + 1).items():
        if name != "x":
            out[name + "_2"] = value
    return out


def reference(
    x, mem, positions, mix_norm_g, mem_norm_g, w_in, w_mem_kv, q_norm_g, k_norm_g, mq_norm_g,
    mk_norm_g, conv_dw_w, conv_dw_b, conv_ln_g, conv_ln_b, w_out, ffn_norm_g, w_up, ffn_dw_w,
    ffn_dw_b, w_down, norm_mix_2, w_in_2, b_forget_2, cmp_pos_2, cmp_w1_2, cmp_b1_2, cmp_w2_2,
    cmp_b2_2, w_o_fox_2, w_o_nsa_2, w_out_2, norm_mlp_2, w_up_2, w_down_2, norm_final_2,
):
    x = first_block(
        x, mem, positions, mix_norm_g, mem_norm_g, w_in, w_mem_kv, q_norm_g, k_norm_g,
        mq_norm_g, mk_norm_g, conv_dw_w, conv_dw_b, conv_ln_g, conv_ln_b, w_out, ffn_norm_g,
        w_up, ffn_dw_w, ffn_dw_b, w_down,
    )
    return second_block(
        x, norm_mix_2, w_in_2, b_forget_2, cmp_pos_2, cmp_w1_2, cmp_b1_2, cmp_w2_2, cmp_b2_2,
        w_o_fox_2, w_o_nsa_2, w_out_2, norm_mlp_2, w_up_2, w_down_2, norm_final_2,
    )


_drawn_inputs = setup_inputs


def setup_inputs(seed=0):
    import zlib

    import numpy as np

    out = dict(_drawn_inputs(seed))
    spreads = {}
    factors = {'mix_norm_g': 6.98,
     'mem_norm_g': 8.0,
     'q_norm_g': 8.0,
     'k_norm_g': 8.0,
     'mq_norm_g': 8.0,
     'mk_norm_g': 8.0,
     'conv_dw_b': 4.167,
     'conv_ln_g': 6.126,
     'conv_ln_b': 7.287,
     'ffn_norm_g': 3.717,
     'ffn_dw_b': 3.722,
     'norm_mix_2': 7.44,
     'b_forget_2': 5.378,
     'cmp_pos_2': 8.0,
     'cmp_b1_2': 8.0,
     'cmp_b2_2': 8.0,
     'norm_mlp_2': 3.831,
     'norm_final_2': 2.867}
    for name, (base, spread) in spreads.items():
        noise = np.random.default_rng([zlib.crc32(name.encode()), seed]).standard_normal(out[name].shape)
        drawn = base * np.exp(spread * noise) if base else spread * noise
        out[name] = __import__('jax').numpy.asarray(drawn.astype(out[name].dtype))
    for name, factor in factors.items():
        out[name] = (out[name] * factor).astype(out[name].dtype)
    return out
```

```python
import numpy as np
import concourse.bass as bass
from concourse import mybir
from contextlib import ExitStack

P = 128
S = 512
D = 1024
DC = D // P
HD = 64
NMEM = 256
CONV_K, CONV_W = 31, 256
HALO = CONV_K // 2
FF1, FF2 = 2816, 4096
LAYERS = 2
CMP_LEN, CMP_STEP = 32, 16
NCMP = (S - CMP_LEN) // CMP_STEP + 1
EPS = 1e-6
BIG = 1e30
TT = S // P

RING = 3
B_IN1, B_MEM, B_OUT1, B_UP1, B_DOWN1 = 0, 18, 22, 30, 74
DOWN1_BLOCKS = 3
B_L = B_DOWN1 + DC * DOWN1_BLOCKS
IN2, TURNS, GATES, BOTH, OUT2, UPDOWN = 0, 7, 31, 47, 55, 63
LAYER_BLOCKS = UPDOWN + 64
NBLOCKS = B_L + LAYERS * LAYER_BLOCKS

_PAR = [("mix_g", 8), ("mem_g", 8), ("ffn_g", 8), ("q_g", 1), ("k_g", 1), ("mq_g", 1), ("mk_g", 1),
        ("conv_w", 2 * CONV_K), ("conv_b", 2), ("ln_g", 2), ("ln_b", 2), ("ffn_w", 44 * 3),
        ("ffn_b", 44), ("inv_freq", 1), ("eps", 1), ("eps64", 1), ("norm_final", 8)]
for _l in range(LAYERS):
    _PAR += [(f"norm_mix{_l}", 8), (f"norm_mlp{_l}", 8), (f"fgate_b{_l}", 1), (f"pos_k{_l}", 16),
             (f"pos_v{_l}", 16), (f"b1_k{_l}", 2), (f"b1_v{_l}", 2), (f"b2_k{_l}", 1), (f"b2_v{_l}", P),
             (f"w2_k{_l}", 2 * P), (f"w2_v{_l}", P)]
PAR, _at = {}, 0
for _n, _w in _PAR:
    PAR[_n] = (_at, _w)
    _at += _w
NPAR = _at


def build(nc, xT, memT, positions, wstream, params, fconst, bconst, lncount, trig2, out):
    dt = mybir.dt
    f32, f32r, bf16 = dt.float32, dt.float32r, dt.bfloat16
    ALU, ACT, AX = mybir.AluOpType, mybir.ActivationFunctionType, mybir.AxisListType
    ctx = ExitStack()
    with ctx:
        KIB = 1024
        base = 16512

        def at(name, shape, dtype, offset):
            return nc.alloc_sbuf_tensor_at(name, [P, *shape], dtype, offset=base + offset)

        def sem(name):
            return ctx.enter_context(nc.semaphore(name))

        w_raw = at("w_raw", [RING, 1024], f32, 0)
        w_hi = at("w_hi", [RING, 1024], f32r, 12 * KIB)
        w_lo = at("w_lo", [RING, 1024], f32r, 24 * KIB)
        x = at("x", [DC, S], f32, 36 * KIB)
        hn_hi = at("hn_hi", [DC, S], f32r, 52 * KIB)
        hn_lo = at("hn_lo", [DC, S], f32r, 68 * KIB)
        R = 84 * KIB
        q1 = at("q1", [4, S], f32, R)
        k1 = at("k1", [4, 2, S], f32, R + 8 * KIB)
        v1 = at("v1", [TT, 512], f32, R + 24 * KIB)
        qm = at("qm", [2, S], f32, R + 32 * KIB)
        km = at("km", [2, 2, NMEM], f32, R + 36 * KIB)
        vm = at("vm", [2, 256], f32, R + 40 * KIB)
        conv_in = at("conv_in", [2, S + 2 * HALO], f32, R + 42 * KIB)
        conv_acc = at("conv_acc", [2, S], f32, R + 47 * KIB)
        o1 = at("o1", [TT, 768], f32, R + 51 * KIB)
        lnc = at("lnc", [TT, S], f32, R + 67 * KIB)
        srow = at("srow", [2, S], f32, R + 75 * KIB)
        vt1 = at("vt1", [2, S], f32, R + 75 * KIB)
        cos1 = at("cos1", [S], f32, R + 79 * KIB)
        sin1 = at("sin1", [S], f32, R + 81 * KIB)
        mem_x = at("mem_x", [DC, NMEM], f32, R)
        mn_hi = at("mn_hi", [DC, NMEM], f32r, R + 51 * KIB)
        mn_lo = at("mn_lo", [DC, NMEM], f32r, R + 59 * KIB)
        angle = at("angle", [3, S], f32, R + 8 * KIB)
        pos_i = at("pos_i", [S], dt.int32, R + 14 * KIB)
        pos_f = at("pos_f", [S], f32, R + 16 * KIB)
        mix_hi = at("mix_hi", [DC, S], f32r, 52 * KIB)
        mix_lo = at("mix_lo", [DC, S], f32r, 68 * KIB)
        hid1_hi = at("hid1_hi", [22, S], f32r, R)
        hid1_lo = at("hid1_lo", [22, S], f32r, R + 44 * KIB)
        qa = at("qa", [4, S], f32, R)
        ka = at("ka", [4, 2, S], f32, R + 8 * KIB)
        va = at("va", [TT, 512], f32, R + 24 * KIB)
        qb = at("qb", [4, S], f32, R + 32 * KIB)
        ksw = at("ksw", [2, 2, S], f32, R + 40 * KIB)
        vsw = at("vsw", [2, TT, P], f32, R + 48 * KIB)
        kc = at("kc", [2, NCMP], f32, R + 52 * KIB)
        vbd = at("vbd", [2, 256], f32, R + 52 * KIB + 512)
        hidc = at("hidc", [2, 2, 62], f32, R + 54 * KIB + 512)
        gates = at("gates", [TT, 24], f32, R + 55 * KIB + 512)
        c3 = at("c3", [S], bf16, R + 56 * KIB)
        lf = at("lf", [TT, 8], f32, R + 57 * KIB)
        fgs = at("fgs", [S], f32, R + 57 * KIB + 128)
        z32 = at("z32", [3, TT, 32], f32, R + 59 * KIB + 256)
        s8 = at("s8", [5, TT, 8], f32, R + 60 * KIB + 896)
        oa = at("oa", [TT, 512], f32, R + 66 * KIB)
        on = at("on", [TT, 512], f32, R + 74 * KIB)
        cmp_t = at("cmp_t", [2, S], f32, R + 66 * KIB)
        cmp_g = at("cmp_g", [2, 1024], f32, R + 70 * KIB)
        cs2 = at("cs2", [2, S], f32, R + 82 * KIB)
        sg = at("sg", [2 * DC, S], f32, R)
        mx = at("mx", [DC, 2, S], f32r, R)
        mx_hi, mx_lo = mx[:, :, 0, :], mx[:, :, 1, :]
        ya_hi = at("ya_hi", [4, S], f32r, R + 32 * KIB)
        ya_lo = at("ya_lo", [4, S], f32r, R + 40 * KIB)
        yn_hi = at("yn_hi", [4, S], f32r, R + 48 * KIB)
        yn_lo = at("yn_lo", [4, S], f32r, R + 56 * KIB)
        mt = at("mt", [2, S], f32, R + 74 * KIB)
        hid_hi = at("hid_hi", [16, S], f32r, R)
        hid_lo = at("hid_lo", [16, S], f32r, R + 32 * KIB)
        T = R + 88 * KIB
        sq = at("sq", [2, S], f32, T)
        rt = at("rt", [S], f32, T + 4 * KIB)
        ri = at("ri", [S], f32, T + 6 * KIB)
        tmp = at("tmp", [3, S], f32, T + 8 * KIB)
        t1 = at("t1", [S], f32, T + 14 * KIB)
        mid_b = at("mid_b", [S], bf16, T + 6 * KIB)
        prow = at("prow", [3, S], f32, T)
        pT = at("pT", [2, S], f32, T + 6 * KIB)
        crow = at("crow", [TT, 256], f32, T)
        cprob = at("cprob", [TT, 8, 32], f32, T + 4 * KIB)
        cprobT = at("cprobT", [TT, 256], f32, T + 8 * KIB)
        yrow = at("yrow", [4, S], f32, T)
        yout = at("yout", [DC, S], f32, 52 * KIB)
        Q = T + 16 * KIB
        par = at("par", [NPAR], f32, Q)
        Q += (NPAR * 4 + 31) // 32 * 32
        fc = at("fc", [5 * P + S + 32], f32, Q)
        Q += (5 * P + S + 32) * 4
        bc = at("bc", [2 * P + 4 * 248 + 8 * P], bf16, Q)
        Q += (2 * P + 4 * 248 + 8 * P) * 2
        neg_g = at("neg_g", [2], f32, Q)
        zero = at("zero", [1], f32, Q + 32 + 1024 + 512)
        cols = at("cols", [4, 64], f32, Q + 32)
        cmpc = at("cmpc", [4, TT, 8], f32, Q + 32 + 1024)
        assert base + Q + 64 + 1024 + 512 <= nc.sbuf_usable_end
        ident, rot, headmean, mean1024, mean256 = (fc[:, i * P:(i + 1) * P] for i in range(5))
        tri = fc[:, 5 * P:5 * P + S]
        valid0 = fc[:, 5 * P + S:5 * P + S + NCMP]
        identb, causal = bc[:, 0:P], bc[:, P:2 * P]
        cmask = bc[:, 2 * P:2 * P + 4 * 248].rearrange("p (t n) -> p t n", t=4)
        headsel = bc[:, 2 * P + 4 * 248:].rearrange("p (h n) -> p h n", h=8)

        def pcol(name, i=0, n=1):
            a = PAR[name][0] + i
            return par[:, a:a + n]

        ps = [ctx.enter_context(nc.psum_tensor(f"bank{i}", [P, S], f32)) for i in range(8)]

        w_loaded = [sem(f"w_loaded{i}") for i in range(RING)]
        zero_set, w_rounded, w_split, blocks_done = sem("zero_set"), sem("w_rounded"), sem("w_split"), sem("blocks_done")
        x_loaded = [sem(f"x_loaded{n}") for n in range(4)]
        mem_loaded, par_loaded, mask_loaded, pos_loaded, lnc_loaded = (
            sem(n) for n in ("mem_loaded", "par_loaded", "mask_loaded", "pos_loaded", "lnc_loaded"))
        norm_sq, norm_sum, norm_rt, norm_full, norm_hi, norm_lo = (
            sem(n) for n in ("norm_sq", "norm_sum", "norm_rt", "norm_full", "norm_hi", "norm_lo"))
        act_took, dve_took, dve_chain, act_chain = (
            sem(n) for n in ("act_took", "dve_took", "dve_chain", "act_chain"))
        qk_sq, qk_sum, qk_rt = sem("qk_sq"), sem("qk_sum"), sem("qk_rt")
        rotated, roped, v_turned, v_kept = sem("rotated"), sem("roped"), sem("v_turned"), sem("v_kept")
        trig_angle, trig_ready = sem("trig_angle"), sem("trig_ready")
        scored, row_min, row_exp, p_turned, p_kept, pv_done, o_kept = (
            sem(n) for n in ("scored", "row_min", "row_exp", "p_turned", "p_kept", "pv_done", "o_kept"))
        conv_taps, ln_sum, ln_centred, ln_sq, ln_rt, ln_full, ln_hi, ln_lo = (
            sem(n) for n in ("conv_taps", "ln_sum", "ln_centred", "ln_sq", "ln_rt", "ln_full", "ln_hi", "ln_lo"))
        o_turned, o_hi, o_lo = sem("o_turned"), sem("o_hi"), sem("o_lo")
        ff_lin, ff_silu, ff_full, ff_hi, ff_lo = (
            sem(n) for n in ("ff_lin", "ff_silu", "ff_full", "ff_hi", "ff_lo"))
        mix_full, mix_rounded, mix_split = sem("mix_full"), sem("mix_rounded"), sem("mix_split")
        fg_turned, fg_abs, fg_exp, fg_log, fg_cum, fg_parts = (
            sem(n) for n in ("fg_turned", "fg_abs", "fg_exp", "fg_log", "fg_cum", "fg_parts"))
        cmp_full, cmp_out, cmp_biased, cmp_rot, cmp_kept = (
            sem(n) for n in ("cmp_full", "cmp_out", "cmp_biased", "cmp_rot", "cmp_kept"))
        c_scored, c_shift, c_exp, c_prob, c_turned, c_kept, c_pv, c_o = (
            sem(n) for n in ("c_scored", "c_shift", "c_exp", "c_prob", "c_turned", "c_kept", "c_pv", "c_o"))
        trig2_loaded, out_full, out_stored = sem("trig2_loaded"), sem("out_full"), sem("out_stored")

        tiles, taken = [], {"act": 0, "dve": 0}
        TAKER = {"q": "dve", "k": "dve", "qm": "dve", "km": "dve", "v": "act", "vm": "act", "ga": "dve",
                 "gg": "act", "add": "dve", "fg": "dve", "fu": "dve", "cp": "act", "kz": "act",
                 "gate": "act", "qr": "act", "kr": "act", "cmp": "act", "w1": "act", "sig": "act",
                 "fox": "dve", "nsa": "dve", "relu": "act"}

        def tile(kind, i, block, n, bank=None):
            who = TAKER[kind]
            taken[who] += 1
            tiles.append((kind, i, block, n, len(tiles) % 4 if bank is None else bank, who, taken[who]))
            return len(tiles) - 1

        b = B_IN1
        IN1 = []
        for kind, n in (("q", 4), ("k", 4), ("v", 4)):
            for i in range(n):
                IN1.append(tile(kind, i, b, 1)); b += 1
        for i in range(2):
            IN1.append(tile("ga", i, B_IN1 + 12 + 2 * i, 1))
            IN1.append(tile("gg", i, B_IN1 + 13 + 2 * i, 1))
        b = B_IN1 + 16
        for kind, n in (("qm", 2), ("km", 2), ("vm", 2)):
            for i in range(n):
                IN1.append(tile(kind, i, b, 1)); b += 1
        OUT1 = [tile("add", m, B_OUT1 + m, 1) for m in range(DC)]
        UP1 = [tile(("fg", "fu")[i % 2], i // 2, B_UP1 + i, 1) for i in range(44)]
        DN1 = [tile("add", m, B_DOWN1 + DOWN1_BLOCKS * m, DOWN1_BLOCKS) for m in range(DC)]
        HEAD2 = [("cmp", 0), ("cmp", 1), ("gate", 0)] + [("kz", i) for i in range(4)]
        TURN2 = [[("cp", i) for i in range(4)], [("v", i) for i in range(4)], [("qr", i) for i in range(4)],
                 [("kr", 0), ("kr", 1), ("v", 4), ("v", 5)]]
        LIN = []
        for l in range(LAYERS):
            o = B_L + l * LAYER_BLOCKS
            ph = {"in": [tile(k, i, o + IN2 + n, 1) for n, (k, i) in enumerate(HEAD2)]}
            for n, four in enumerate(TURN2):
                c = o + TURNS + 6 * n
                ph["in"].append(tile("w1", n, c, 2))
                ph["in"] += [tile(k, i, c + 2 + m, 1) for m, (k, i) in enumerate(four)]
            ph["cmp"] = [t for t in ph["in"] if tiles[t][0] == "w1"]
            ph["gates"] = [tile("sig", n, o + GATES + n, 1, 3) for n in range(16)]
            ph["mix"] = [[tile(k, m, o + BOTH + m, 1, 2 * (m % 3) + n) for n, k in enumerate(("fox", "nsa"))]
                         for m in range(DC)]
            ph["out"] = [tile("add", m, o + OUT2 + m, 1) for m in range(DC)]
            for half in range(2):
                u = o + UPDOWN + 32 * half
                ph[f"up{half}"] = [tile("relu", i, u + i, 1) for i in range(16)]
                ph[f"down{half}"] = [tile("add", m, u + 16 + 2 * m, 2) for m in range(DC)]
            LIN.append(ph)

        def filled(t):
            return tiles[t][2] + tiles[t][3]

        def took(t):
            return (act_took if tiles[t][5] == "act" else dve_took), tiles[t][6]

        NORM_AFTER = {2: OUT1, 3: DN1, 4: LIN[0]["out"], 5: LIN[0]["down1"], 6: LIN[1]["out"], 7: LIN[1]["down1"]}
        NORM_G = {0: "mix_g", 1: "mem_g", 2: "ffn_g", 3: "norm_mix0", 4: "norm_mlp0", 5: "norm_mix1",
                  6: "norm_mlp1", 7: "norm_final"}

        U1 = [("b1", h, t) for h in range(8) for t in range(TT)] + [("mem", h, t) for h in range(4) for t in range(TT)]
        UF = [("fox", h, t) for h in range(8) for t in range(TT)]
        UN = [(k, h, t) for k in ("sel", "win") for h in range(8) for t in range(TT)]
        units, FIRST = list(U1), {"b1": 0}
        for l in range(LAYERS):
            FIRST["fox", l] = len(units)
            units += [u + (l,) for u in UF]
            FIRST["nsa", l] = len(units)
            units += [u + (l,) for u in UN]
        NU = len(units)

        def width(u):
            kind, _, t = units[u][:3]
            return S if kind == "b1" else NMEM if kind == "mem" else P * (t + 1)

        RUNS = [(RING, B_L + TURNS), (B_L + TURNS + 24, B_L + LAYER_BLOCKS + TURNS),
                (B_L + LAYER_BLOCKS + TURNS + 24, NBLOCKS)]

        block = ctx.enter_context(nc.Block())

        @block.sync
        def _(sp):
            for n in range(4):
                sp.dma_start(x[:, 2 * n:2 * n + 2, :], xT[:, 2 * n:2 * n + 2, :]).then_inc(x_loaded[n], 16)
            for s in range(RING):
                sp.dma_start(w_raw[:, s, :], wstream[s]).then_inc(w_loaded[s], 16)
            sp.dma_start(mem_x[:, :, :], memT).then_inc(mem_loaded, 16)

            def load(slot, b, unsplit_before=False):
                if unsplit_before:
                    sp.wait_ge(blocks_done, b + (1 - RING))
                else:
                    sp.wait_ge(w_split, b + (1 - RING))
                sp.dma_start(w_raw[:, slot, :], wstream[b]).then_inc(w_loaded[slot], 16)

            for b0, b1 in RUNS:
                with sp.Fori(0, (b1 - b0) // RING) as turn:
                    for j in range(RING):
                        load((b0 + j) % RING, turn * RING + (b0 + j))
                for b in range(b0 + (b1 - b0) // RING * RING, b1):
                    load(b % RING, b)
                if b1 < NBLOCKS:
                    with sp.Fori(0, 4) as turn:
                        for j in range(6):
                            load((b1 + j) % RING, turn * 6 + (b1 + j), unsplit_before=j in (3, 4))

        @block.gpsimd
        def _(pool):
            def split(slot, loads, b, first=False):
                pool.wait_ge(w_loaded[slot], loads * 16)
                if not first:
                    pool.wait_ge(blocks_done, b + (1 - RING))
                nc.gpsimd.tensor_tensor(w_hi[:, slot, :], w_raw[:, slot, :], zeros,
                                        ALU.add).then_inc(w_rounded, 1)
                pool.wait_ge(w_rounded, b + 1)
                nc.gpsimd.tensor_tensor(w_lo[:, slot, :], w_raw[:, slot, :], w_hi[:, slot, :].bitcast(f32),
                                        ALU.subtract).then_inc(w_split, 1)

            nc.gpsimd.memset(zero[:, :], 0.0).then_inc(zero_set, 1)
            zeros = bass.AP(zero[:, :].tensor, zero[:, :].offset, [zero[:, :].ap[0], [0, 1024]])
            pool.wait_ge(zero_set, 1)
            for s in range(RING):
                split(s, 1, s, first=True)
            for b0, b1 in RUNS:
                with pool.Fori(0, (b1 - b0) // RING) as turn:
                    for j in range(RING):
                        split((b0 + j) % RING, turn + ((b0 + j) // RING + 1), turn * RING + (b0 + j))
                for b in range(b0 + (b1 - b0) // RING * RING, b1):
                    split(b % RING, b // RING + 1, b)
                if b1 < NBLOCKS:
                    with pool.Fori(0, 4) as turn:
                        for j in range(6):
                            slot, loads = (b1 + j) % RING, turn * 2 + ((b1 + j) // RING + 1)
                            if j < 2:
                                pool.wait_ge(w_loaded[slot], loads * 16)
                                pool.wait_ge(w_split, turn * 6 + (b1 + j))
                                pool.sem_inc(w_rounded, 1)
                                pool.sem_inc(w_split, 1)
                            else:
                                split(slot, loads, turn * 6 + (b1 + j))

        @block.tensor
        def _(pe):
            last_on_bank = {}

            def linear(t, hi, lo, cols_, chunks, ready=None, first_chunk=0, last=True, base=0, part=None):
                kind, i, block_, n, bank, _, _ = tiles[t]
                c0, c1 = part or (0, chunks)
                if c0 == 0:
                    if bank in last_on_bank:
                        pe.wait_ge(*took(last_on_bank[bank]))
                    last_on_bank[bank] = t
                for c in range(c0, c1):
                    b_, j = block_ + (c + base) // 8, (c + base) % 8
                    if j == 0 or c == 0:
                        pe.wait_ge(w_split, b_ + 1)
                    if ready is not None:
                        pe.wait_ge(ready[0], ready[1] + c + 1)
                    wh, wl = w_hi[:, b_ % RING, j * P:(j + 1) * P], w_lo[:, b_ % RING, j * P:(j + 1) * P]
                    a_h, a_l = hi[:, first_chunk + c, 0:cols_], lo[:, first_chunk + c, 0:cols_]
                    nc.tensor.matmul(ps[bank][:, 0:cols_], wh, a_h, start=c == 0, stop=False)
                    nc.tensor.matmul(ps[bank][:, 0:cols_], wh, a_l, start=False, stop=False)
                    mm = nc.tensor.matmul(ps[bank][:, 0:cols_], wl, a_h, start=False, stop=c == chunks - 1)
                    if last and (j == 7 or c == chunks - 1):
                        mm.then_inc(blocks_done, 1)

            def linear_w1(t):
                kind, n, block_, _, bank, _, _ = tiles[t]
                pe.wait_ge(*took(last_on_bank[bank]))
                last_on_bank[bank] = t
                for c in range(16):
                    b_, j = block_ + c // 8, c % 8
                    if j == 0:
                        pe.wait_ge(w_split, b_ + 1)
                    mm = nc.tensor.matmul(ps[bank][:, 0:2 * NCMP], w_raw[:, b_ % RING, j * P:(j + 1) * P],
                                          cmp_g[:, n // 2, c * 2 * NCMP:(c + 1) * 2 * NCMP], start=c == 0, stop=c == 15)
                    if j == 7:
                        mm.then_inc(blocks_done, 1)

            def norm(n, cols_=S):
                for c in range(DC):
                    pe.wait_ge(norm_sq, DC * n + c + 1)
                    if c == 0 and n:
                        pe.wait_ge(norm_rt, n)
                    nc.tensor.matmul(ps[7][:, 0:cols_], mean1024, sq[:, c % 2, 0:cols_], start=c == 0,
                                     stop=c == DC - 1).then_inc(norm_sum, 1)

            def turn_tile(src, bank, n, rows=P):
                for t in range(n):
                    mm = nc.tensor.transpose(ps[bank][:, t * rows:(t + 1) * rows], src[0:rows, t * P:(t + 1) * P],
                                             ident[0:rows, 0:rows])
                return mm

            def rotate(n, src, cols_=S):
                if n:
                    pe.wait_ge(roped, n)
                nc.tensor.matmul(ps[5][:, 0:cols_], rot, src, start=True, stop=True).then_inc(rotated, 1)

            def attend(u0, u1, gates_from=None, gate_tiles=()):
                for i in range(u0, u1 + 3):
                    if i < u1:
                        kind, h, t = units[i][:3]
                        bank, w = ps[i % 3], width(i)
                        if i - 3 >= u0:
                            if units[i - 3][0] == "b1":
                                pe.wait_ge(row_min, i - 2)
                            else:
                                pe.wait_ge(row_exp, i - 2)
                        if kind == "b1":
                            q_, k_ = q1[:, h // 2, t * P:(t + 1) * P], k1[:, h // 2, h % 2, :]
                        elif kind == "mem":
                            q_, k_ = qm[:, h // 2, t * P:(t + 1) * P], km[:, h // 2, h % 2, :]
                        elif kind == "fox":
                            q_, k_ = qa[:, h // 2, t * P:(t + 1) * P], ka[:, h // 2, h % 2, 0:w]
                        else:
                            q_ = qb[:, h % 4, t * P:(t + 1) * P]
                            k_ = ksw[:, 0 if kind == "sel" else 1, h // 4, 0:w]
                        plain = kind in ("b1", "mem")
                        mm = nc.tensor.matmul(bank[:, 0:w], q_, k_, start=True, stop=plain)
                        if kind == "fox":
                            nc.tensor.matmul(bank[:, 0:w], headsel[0:96, h, :], c3[0:96, 0:w], start=False, stop=False)
                        if not plain:
                            mm = nc.tensor.matmul(bank[:, t * P:w], identb, causal, start=False, stop=True)
                        mm.then_inc(scored, 1)
                    j = i - 3
                    if j >= u0:
                        kind, h, t = units[j][:3]
                        n = width(j) // P
                        pe.wait_ge(p_kept, j + 1)
                        if j >= 2 and j - 2 >= u0:
                            pe.wait_ge(o_kept, j - 1)
                        for c in range(n):
                            if kind == "b1":
                                v_ = v1[:, c, h * HD:(h + 1) * HD]
                            elif kind == "mem":
                                v_ = vm[:, c, h * HD:(h + 1) * HD]
                            elif kind == "fox":
                                v_ = va[:, c, h * HD:(h + 1) * HD]
                            else:
                                v_ = vsw[:, 0 if kind == "sel" else 1, c, h // 4 * HD:(h // 4 + 1) * HD]
                            mm = nc.tensor.matmul(ps[6 + j % 2][:, 0:HD], pT[:, j % 2, c * P:(c + 1) * P], v_,
                                                  start=c == 0, stop=c == n - 1)
                        mm.then_inc(pv_done, 1)
                    j = i - 2
                    if u0 <= j < u1:
                        pe.wait_ge(row_exp, j + 1)
                        if j - 2 >= u0:
                            pe.wait_ge(p_kept, j - 1)
                        for c in range(width(j) // P):
                            mm = nc.tensor.transpose(ps[4 + j % 2 * 1][:, c * P:(c + 1) * P],
                                                     prow[:, j % 3, c * P:(c + 1) * P], ident)
                        mm.then_inc(p_turned, 1)
                    if gates_from is not None and gates_from <= i < u1:
                        n = 2 * (i - gates_from)
                        linear(gate_tiles[n // 8], hn_hi, hn_lo, S, DC, part=(n % 8, n % 8 + 2))

            def turn_outputs(n0, sources):
                for n, src in enumerate(sources):
                    k = n0 + n
                    if n >= 2:
                        pe.wait_ge(o_lo, k - 1)
                    for t in range(TT):
                        mm = nc.tensor.transpose(ps[4 + n % 2][:, t * P:(t + 1) * P], src[:, t, :], ident)
                    mm.then_inc(o_turned, 1)

            pe.wait_ge(par_loaded, 32)
            norm(0)
            qk, rope_n, v_n = {}, {}, {}
            for t in IN1:
                k = tiles[t][0]
                if k in ("q", "k", "qm", "km"):
                    qk[t] = len(qk)
                if k in ("q", "k"):
                    rope_n[t] = len(rope_n)
                if k in ("v", "vm"):
                    v_n[t] = len(v_n)
            for i in range(len(IN1) + 2):
                if i < len(IN1):
                    t = IN1[i]
                    if tiles[t][0] in ("km", "vm"):
                        linear(t, mn_hi, mn_lo, NMEM, DC, (norm_lo, DC) if tiles[t][:2] == ("km", 0) else None)
                    else:
                        linear(t, hn_hi, hn_lo, S, DC, (norm_lo, 0) if i == 0 else None)
                        if i == 0:
                            norm(1, NMEM)
                if 0 <= i - 1 < len(IN1):
                    t = IN1[i - 1]
                    kind, w = tiles[t][0], NMEM if tiles[t][0] in ("km", "vm") else S
                    if t in qk:
                        pe.wait_ge(qk_sq, qk[t] + 1)
                        if qk[t]:
                            pe.wait_ge(qk_rt, qk[t])
                        nc.tensor.matmul(ps[4][:, 0:w], headmean, sq[:, qk[t] % 2, 0:w], start=True,
                                         stop=True).then_inc(qk_sum, 1)
                    if t in v_n:
                        pe.wait_ge(*took(t))
                        if v_n[t]:
                            pe.wait_ge(v_kept, v_n[t])
                        turn_tile(vt1[:, v_n[t] % 2, :], 6, w // P).then_inc(v_turned, 1)
                if 0 <= i - 2 < len(IN1) and IN1[i - 2] in rope_n:
                    t = IN1[i - 2]
                    pe.wait_ge(*took(t))
                    rotate(rope_n[t], tmp[:, rope_n[t] % 2, :])
            pe.wait_ge(*took(IN1[-3]))
            pe.wait_ge(act_took, tiles[IN1[-1]][6])
            pe.wait_ge(v_kept, len(v_n))
            pe.wait_ge(roped, len(rope_n))
            attend(0, len(U1))
            pe.wait_ge(row_min, len(U1))
            pe.wait_ge(row_exp, len(U1))
            pe.wait_ge(conv_taps, 2 * CONV_K)
            for c in range(2):
                mm = nc.tensor.matmul(ps[0][:, :], mean256, conv_acc[:, c, :], start=c == 0, stop=c == 1)
            mm.then_inc(ln_sum, 1)
            for c in range(2):
                pe.wait_ge(ln_sq, c + 1)
                mm = nc.tensor.matmul(ps[1][:, :], mean256, sq[:, c, :], start=c == 0, stop=c == 1)
            mm.then_inc(ln_sum, 1)
            pe.wait_ge(o_kept, len(U1))
            turn_outputs(0, [o1[:, :, c * P:(c + 1) * P] for c in range(6)])
            pe.wait_ge(o_lo, 6)
            pe.wait_ge(ln_lo, 2)
            for t in OUT1:
                linear(t, mix_hi, mix_lo, S, DC)
            norm(2)
            for n, t in enumerate(UP1):
                linear(t, hn_hi, hn_lo, S, DC, (norm_lo, 2 * DC) if n == 0 else None)
            for n, t in enumerate(DN1):
                linear(t, hid1_hi, hid1_lo, S, 22, (ff_lo, 0) if n == 0 else None)

            roped_n, v_done, turned = len(rope_n), len(v_n), 6
            for l in range(LAYERS):
                ph = LIN[l]
                norm(3 + 2 * l)
                jobs = ph["in"]
                nrot = nv = 0
                for i in range(len(jobs) + 2):
                    if i == 0:
                        pe.wait_ge(mask_loaded, 16)
                    if i < len(jobs) and tiles[jobs[i]][0] == "w1":
                        if tiles[jobs[i]][1] % 2 == 0:
                            pe.wait_ge(cmp_full, 2 * l + tiles[jobs[i]][1] // 2 + 1)
                        linear_w1(jobs[i])
                    elif i < len(jobs):
                        linear(jobs[i], hn_hi, hn_lo, S, DC, (norm_lo, DC * (3 + 2 * l)) if i == 0 else None)
                    if 0 <= i - 1 < len(jobs):
                        t = jobs[i - 1]
                        kind = tiles[t][0]
                        if kind in ("qr", "kr"):
                            pe.wait_ge(*took(t))
                            rotate(roped_n, tmp[:, roped_n % 2, :])
                            roped_n += 1
                        if kind == "v":
                            pe.wait_ge(*took(t))
                            pe.wait_ge(v_kept, v_done)
                            turn_tile(sq[:, v_done % 2, :], 6, TT).then_inc(v_turned, 1)
                            v_done += 1
                        if kind == "gate":
                            pe.wait_ge(*took(t))
                            turn_tile(fgs[:, :], 4, TT, 32).then_inc(fg_turned, 1)
                    if 0 <= i - 2 < len(jobs) and tiles[jobs[i - 2]][0] == "gate":
                        pe.wait_ge(fg_log, l + 1)
                        for t in range(TT):
                            mm = nc.tensor.matmul(ps[4][0:8, t * P:S], lf[:, t, :], tri[:, 0:S - t * P],
                                                  start=t == 0, stop=t == TT - 1)
                        mm.then_inc(fg_cum, 1)
                pe.wait_ge(*took(ph["cmp"][1]))
                pe.wait_ge(fg_parts, l + 1)
                for g in range(2):
                    for f in range(2):
                        mm = nc.tensor.matmul(ps[4][:, g * NCMP:(g + 1) * NCMP], pcol(f"w2_k{l}", f * P, P),
                                              hidc[:, 0, f, g * NCMP:(g + 1) * NCMP], start=f == 0, stop=f == 1)
                mm.then_inc(cmp_out, 1)
                pe.wait_ge(*took(ph["cmp"][3]))
                pe.wait_ge(v_kept, v_done)
                for g in range(2):
                    for f in range(2):
                        mm = nc.tensor.matmul(ps[6][0:NCMP, g * HD:(g + 1) * HD], hidc[:, 1, f, g * NCMP:(g + 1) * NCMP],
                                              pcol(f"w2_v{l}", f * HD, HD), start=f == 0, stop=f == 1)
                mm.then_inc(cmp_out, 1)
                pe.wait_ge(cmp_biased, l + 1)
                pe.wait_ge(roped, roped_n)
                nc.tensor.matmul(ps[5][:, 0:2 * NCMP], rot, t1[:, 0:2 * NCMP], start=True,
                                 stop=True).then_inc(cmp_rot, 1)
                pe.wait_ge(cmp_kept, 2 * (l + 1))
                for t in range(TT):
                    nc.tensor.matmul(ps[t][:, 0:8 * NCMP], identb, cmask[:, t, :], start=True, stop=False)
                    for slot in range(8):
                        mm = nc.tensor.matmul(ps[t][:, slot * NCMP:(slot + 1) * NCMP], qb[:, slot % 4, t * P:(t + 1) * P],
                                              kc[:, slot // 4, :], start=False, stop=slot == 7)
                    mm.then_inc(c_scored, 1)
                for t in range(TT):
                    pe.wait_ge(c_prob, TT * l + t + 1)
                    if t >= 2:
                        pe.wait_ge(c_kept, TT * l + t - 1)
                    for g in range(2):
                        a = g * P
                        mm = nc.tensor.transpose(ps[4 + t % 2][:, a:a + P],
                                                 cprob[:, t, 4 * g:4 * g + 4, :].rearrange("p a b -> p (a b)"), ident)
                    mm.then_inc(c_turned, 1)
                for t in range(TT):
                    pe.wait_ge(c_kept, TT * l + t + 1)
                    if t >= 2:
                        pe.wait_ge(c_o, TT * l + t - 1)
                    for g in range(2):
                        mm = nc.tensor.matmul(ps[6 + t % 2][:, g * 256:(g + 1) * 256], cprobT[:, t, g * P:(g + 1) * P],
                                              vbd[:, g, :], start=True, stop=True)
                    mm.then_inc(c_pv, 1)
                pe.wait_ge(c_shift, TT * (l + 1))
                pe.wait_ge(c_o, TT * (l + 1))
                pe.wait_ge(v_kept, v_done)
                u0, u1 = FIRST["fox", l], FIRST["nsa", l] + len(UN)
                attend(u0, u1, FIRST["nsa", l], ph["gates"])
                pe.wait_ge(o_kept, u1)
                pe.wait_ge(p_kept, u1)
                turn_outputs(turned, [oa[:, :, c * P:(c + 1) * P] for c in range(4)]
                             + [on[:, :, c * P:(c + 1) * P] for c in range(4)])
                turned += 8
                for m in range(DC):
                    fox_, nsa_ = ph["mix"][m]
                    if m == 0:
                        pe.wait_ge(o_lo, turned - 4)
                    linear(fox_, ya_hi, ya_lo, S, 4, last=False)
                    if m == 0:
                        pe.wait_ge(o_lo, turned)
                    linear(nsa_, yn_hi, yn_lo, S, 4, base=4)
                for n, t in enumerate(ph["out"]):
                    linear(t, mx_hi, mx_lo, S, DC, (mix_split, DC * l) if n == 0 else None)
                norm(4 + 2 * l)
                for half in range(2):
                    for n, t in enumerate(ph[f"up{half}"]):
                        linear(t, hn_hi, hn_lo, S, DC, (norm_lo, DC * (4 + 2 * l)) if half == n == 0 else None)
                    for n, t in enumerate(ph[f"down{half}"]):
                        linear(t, hid_hi, hid_lo, S, 16, (ff_lo, 22 + 32 * l + 16 * half) if n == 0 else None)
            norm(7)

        @block.scalar
        def _(act):
            A = nc.scalar.activation
            act.dma_start(par[:, :], params).then_inc(par_loaded, 16)
            act.dma_start(fc[:, :], fconst).then_inc(par_loaded, 16)
            act.dma_start(pos_i[:, :], positions.to_broadcast([P, S])).then_inc(pos_loaded, 16)
            act.wait_ge(par_loaded, 32)

            def norm(n, src, hi, cols_=S):
                for c in range(DC):
                    if n == 0 and c % 2 == 0:
                        act.wait_ge(x_loaded[c // 2], 16)
                    if n in NORM_AFTER:
                        act.wait_ge(dve_took, tiles[NORM_AFTER[n][c]][6])
                    if DC * n + c >= 2:
                        act.wait_ge(norm_sum, DC * n + c - 1)
                    A(sq[:, c % 2, 0:cols_], src[:, c, :], ACT.Square).then_inc(norm_sq, 1)
                act.wait_ge(norm_sum, DC * (n + 1))
                A(rt[:, 0:cols_], ps[7][:, 0:cols_], ACT.Sqrt, bias=pcol("eps")).then_inc(norm_rt, 1)
                if hi is None:
                    return
                for c in range(DC):
                    act.wait_ge(norm_full, DC * n + c + 1)
                    A(hi[:, c, :], tmp[:, c % 3, 0:cols_], ACT.Copy).then_inc(norm_hi, 1)

            def attend(u0, u1, gates_from=None, gate_tiles=()):
                for i in range(u0, u1 + 2):
                    g = None if gates_from is None else (i - gates_from) // 4 - 1
                    if g is not None and g >= 0 and (i - gates_from) % 4 == 0:
                        t = gate_tiles[g]
                        act.wait_ge(blocks_done, filled(t))
                        if g == 0:
                            act.wait_ge(pv_done, gates_from)
                        A(sg[:, g, :], ps[3][:, :], ACT.Exp, scale=-1.0).then_inc(act_took, 1)
                    j = i - 2
                    if j >= u0:
                        w = width(j)
                        act.wait_ge(p_turned, j + 1)
                        if j - 2 >= u0:
                            act.wait_ge(pv_done, j - 1)
                        A(pT[:, j % 2, 0:w], ps[4 + j % 2][:, 0:w], ACT.Copy).then_inc(p_kept, 1)
                    if i < u1:
                        kind, w = units[i][0], width(i)
                        act.wait_ge(row_min, i + 1)
                        if i - 3 >= u0:
                            act.wait_ge(p_turned, i - 2)
                        src = srow[:, i % 2, :] if kind == "b1" else ps[i % 3][:, 0:w]
                        A(prow[:, i % 3, 0:w], src, ACT.Exp, scale=-1.0, bias=cols[:, 0, i % 64:i % 64 + 1],
                          accum_out=cols[:, 1, i % 64:i % 64 + 1]).then_inc(row_exp, 1)

            def keep_turned(n0, dests):
                for n, d in enumerate(dests):
                    act.wait_ge(o_turned, n0 + n + 1)
                    A(d, ps[4 + n % 2][:, :], ACT.Copy).then_inc(o_hi, 1)

            norm(0, x, hn_hi)
            act.dma_start(lnc[:, :, :], lncount).then_inc(lnc_loaded, 16)
            act.dma_start(bc[:, :], bconst).then_inc(mask_loaded, 16)
            act.wait_ge(mem_loaded, 16)
            norm(1, mem_x, mn_hi, NMEM)
            act.wait_ge(trig_angle, 1)
            A(sin1[:, :], angle[:, 0, :], ACT.Sin).then_inc(trig_ready, 1)
            A(cos1[:, :], angle[:, 1, :], ACT.Sin).then_inc(trig_ready, 1)
            e_of, v_of, e, v = {}, {}, 0, 0
            for t in IN1:
                if tiles[t][0] in ("q", "k", "qm", "km"):
                    e_of[t] = e; e += 1
                if tiles[t][0] in ("v", "vm"):
                    v_of[t] = v; v += 1
            last_normed = None
            for i in range(len(IN1) + 1):
                if i < len(IN1):
                    t = IN1[i]
                    kind, _, _, _, bank = tiles[t][:5]
                    w = NMEM if kind in ("km", "vm") else S
                    act.wait_ge(blocks_done, filled(t))
                    if t in e_of:
                        if e_of[t] >= 2:
                            act.wait_ge(qk_sum, e_of[t] - 1)
                        A(sq[:, e_of[t] % 2, 0:w], ps[bank][:, 0:w], ACT.Square).then_inc(qk_sq, 1)
                    elif t in v_of:
                        if v_of[t] >= 2:
                            act.wait_ge(v_turned, v_of[t] - 1)
                        A(vt1[:, v_of[t] % 2, 0:w], ps[bank][:, 0:w], ACT.Copy).then_inc(act_took, 1)
                    elif kind == "gg":
                        if tiles[t][1]:
                            act.wait_ge(*took(IN1[i - 3]))
                        A(tmp[:, 2, :], ps[bank][:, :], ACT.Sigmoid).then_inc(act_took, 1)
                if i >= 1:
                    t = IN1[i - 1]
                    kind, idx = tiles[t][:2]
                    w = NMEM if kind in ("km", "vm") else S
                    if t in e_of:
                        act.wait_ge(qk_sum, e_of[t] + 1)
                        if last_normed is not None:
                            act.wait_ge(*took(last_normed))
                        last_normed = t
                        q_like = kind in ("q", "qm")
                        A(rt[:, 0:w], ps[4][:, 0:w], ACT.Sqrt, scale=64.0 if q_like else 1.0,
                          bias=pcol("eps64" if q_like else "eps")).then_inc(qk_rt, 1)
                    if t in v_of:
                        act.wait_ge(v_turned, v_of[t] + 1)
                        d = (v1[:, :, idx * P:(idx + 1) * P] if kind == "v" else vm[:, :, idx * P:(idx + 1) * P])
                        A(d, ps[6][:, 0:w].rearrange("p (t n) -> p t n", n=P), ACT.Copy).then_inc(v_kept, 1)
            attend(0, len(U1))
            for c in range(2):
                act.wait_ge(ln_centred, c + 1)
                A(sq[:, c, :], conv_acc[:, c, :], ACT.Square).then_inc(ln_sq, 1)
            act.wait_ge(ln_sum, 2)
            A(rt[:, :], ps[1][:, :], ACT.Sqrt, bias=pcol("eps")).then_inc(ln_rt, 1)
            keep_turned(0, [mix_hi[:, c, :] for c in (0, 1, 2, 3, 6, 7)])
            for c in range(2):
                act.wait_ge(ln_full, c + 1)
                A(tmp[:, c, :], tmp[:, c, :], ACT.Silu, bias=pcol("ln_b", c)).then_inc(act_chain, 1)
                act.wait_ge(act_chain, c + 1)
                A(mix_hi[:, 4 + c, :], tmp[:, c, :], ACT.Copy).then_inc(ln_hi, 1)
            norm(2, x, hn_hi)
            for j in range(22):
                for k in range(2):
                    t = UP1[2 * j + k]
                    ch = j + 22 * k
                    act.wait_ge(blocks_done, filled(t))
                    if j >= 2:
                        act.wait_ge(ff_full, j - 1)
                    A(yrow[:, (2 * j + k) % 4, :], ps[tiles[t][4]][:, :], ACT.Identity, scale=pcol("ffn_w", 3 * ch + 1),
                      bias=pcol("ffn_b", ch)).then_inc(ff_lin, 1)
                act.wait_ge(*took(UP1[2 * j]))
                A(yrow[:, (2 * j) % 4, :], yrow[:, (2 * j) % 4, :], ACT.Silu).then_inc(ff_silu, 1)
                act.wait_ge(ff_full, j + 1)
                A(hid1_hi[:, j, :], tmp[:, j % 3, :], ACT.Copy).then_inc(ff_hi, 1)

            roped_n, v_done, turned = 8, 6, 6
            for l in range(LAYERS):
                ph = LIN[l]
                act.wait_ge(blocks_done, B_L + l * LAYER_BLOCKS)
                act.dma_start(cs2[:, :, :], trig2).then_inc(trig2_loaded, 16)
                norm(3 + 2 * l, x, hn_hi)
                jobs = ph["in"]
                for i in range(len(jobs) + 1):
                    if i < len(jobs):
                        t = jobs[i]
                        kind, idx, _, _, bank = tiles[t][:5]
                        act.wait_ge(blocks_done, filled(t))
                        src = ps[bank]
                        if kind == "w1":
                            A(hidc[:, idx // 2, idx % 2, :], src[:, 0:2 * NCMP], ACT.Gelu_apprx_tanh,
                              bias=pcol(f"b1_{'kv'[idx // 2]}{l}", idx % 2)).then_inc(act_took, 1)
                        elif kind == "cp":
                            A(qa[:, idx, :], src[:, :], ACT.Copy, scale=-0.125).then_inc(act_took, 1)
                        elif kind == "kz":
                            A(ka[0:64, idx, 0, :], src[0:64, :], ACT.Copy)
                            A(ka[64:128, idx, 1, :], src[64:128, :], ACT.Copy).then_inc(act_took, 1)
                        elif kind == "v":
                            vi = v_done + idx
                            act.wait_ge(v_turned, vi - 1)
                            A(sq[:, vi % 2, :], src[:, :], ACT.Copy).then_inc(act_took, 1)
                        elif kind == "gate":
                            A(fgs[0:32, :], src[0:32, :], ACT.Identity, bias=par[0:32, PAR[f"fgate_b{l}"][0]:PAR[f"fgate_b{l}"][0] + 1]).then_inc(act_took, 1)
                        elif kind in ("qr", "kr"):
                            rn = roped_n + idx + (4 if kind == "kr" else 0)
                            act.wait_ge(roped, rn - 1)
                            A(tmp[:, rn % 2, :], src[:, :], ACT.Copy,
                              scale=-0.125 if kind == "qr" else 1.0).then_inc(act_took, 1)
                        elif kind == "cmp":
                            if idx:
                                act.wait_ge(cmp_full, 2 * l + 1)
                            for g in range(2):
                                A(cmp_t[0:64, g, :], src[64 * g:64 * g + 64, :], ACT.Copy)
                                ins = A(cmp_t[64:128, g, 0:S - 1], src[64 * g:64 * g + 64, 1:S], ACT.Copy)
                            ins.then_inc(act_took, 1)
                    if i >= 1:
                        t = jobs[i - 1]
                        kind, idx = tiles[t][:2]
                        if kind == "v":
                            vi = v_done + idx
                            act.wait_ge(v_turned, vi + 1)
                            d = va[:, :, idx * P:(idx + 1) * P] if idx < 4 else vsw[:, idx - 4, :, :]
                            A(d, ps[6][:, :].rearrange("p (t n) -> p t n", n=P), ACT.Copy).then_inc(v_kept, 1)
                        if kind == "gate":
                            act.wait_ge(fg_abs, l + 1)
                            A(z32[:, 2, :, :], z32[:, 1, :, :], ACT.Exp, scale=-1.0).then_inc(fg_exp, 1)
                roped_n += 6
                v_done += 6
                for t in range(TT):
                    act.wait_ge(c_shift, TT * l + t + 1)
                    A(cprob[:, t, :, 0:NCMP], crow[:, t, 0:8 * NCMP].rearrange("p (h n) -> p h n", h=8), ACT.Exp,
                      scale=-1.0).then_inc(c_exp, 1)
                for t in range(TT):
                    act.wait_ge(c_turned, TT * l + t + 1)
                    A(cprobT[:, t, :], ps[4 + t % 2][:, 0:256], ACT.Copy).then_inc(c_kept, 1)
                act.wait_ge(c_pv, TT * (l + 1))
                attend(FIRST["fox", l], FIRST["nsa", l] + len(UN), FIRST["nsa", l], ph["gates"])
                act.wait_ge(pv_done, FIRST["nsa", l] + len(UN))
                keep_turned(turned, [ya_hi[:, c, :] for c in range(4)] + [yn_hi[:, c, :] for c in range(4)])
                turned += 8
                for m in range(DC):
                    act.wait_ge(mix_full, DC * l + m + 1)
                    A(mx_hi[:, m, :], tmp[:, m % 3, :], ACT.Copy).then_inc(mix_rounded, 1)
                norm(4 + 2 * l, x, hn_hi)
                for half in range(2):
                    for i, t in enumerate(ph[f"up{half}"]):
                        n = 22 + 32 * l + 16 * half + i
                        act.wait_ge(blocks_done, filled(t))
                        act.wait_ge(ff_lo, n - 2)
                        if half and i == 0:
                            act.wait_ge(blocks_done, filled(ph["down0"][-1]))
                        A(tmp[:, n % 3, :], ps[tiles[t][4]][:, :], ACT.Relu).then_inc(act_took, 1)
                        act.wait_ge(*took(t))
                        A(hid_hi[:, i, :], tmp[:, n % 3, :], ACT.Square).then_inc(ff_hi, 1)
            norm(7, x, None)
            for c in range(DC):
                act.wait_ge(out_full, c + 1)
                act.dma_start(out[:, c, :], yout[:, c, :]).then_inc(out_stored, 16)
            act.wait_ge(out_stored, 16 * DC)

        @block.vector
        def _(dve):
            V = nc.vector
            chain = [0]

            def link(ins):
                chain[0] += 1
                ins.then_inc(dve_chain, 1)
                dve.wait_ge(dve_chain, chain[0])

            def norm(n, src, hi, lo, cols_=S):
                dve.wait_ge(norm_rt, n + 1)
                link(V.reciprocal(ri[:, 0:cols_], rt[:, 0:cols_]))
                for c in range(DC + 1):
                    if c < DC:
                        if c >= 3 and hi is not None:
                            dve.wait_ge(norm_lo, DC * n + c - 2)
                        d = tmp[:, c % 3, 0:cols_] if hi is not None else yout[:, c, :]
                        V.scalar_tensor_tensor(out=d, in0=src[:, c, :], scalar=pcol(NORM_G[n], c), in1=ri[:, 0:cols_],
                                               op0=ALU.mult, op1=ALU.mult).then_inc(norm_full if hi is not None else out_full, 1)
                    if c and hi is not None:
                        dve.wait_ge(norm_full, DC * n + c)
                        dve.wait_ge(norm_hi, DC * n + c)
                        V.tensor_tensor(lo[:, c - 1, :], tmp[:, (c - 1) % 3, 0:cols_], hi[:, c - 1, :].bitcast(f32),
                                        ALU.subtract).then_inc(norm_lo, 1)

            taps = [0]

            def conv_tap():
                n = taps[0]
                if n == 2 * CONV_K:
                    return
                taps[0] += 1
                c, k = n % 2, n // 2
                src, w = conv_in[:, c, k:k + S], pcol("conv_w", c * CONV_K + k)
                if k == 0:
                    ins = V.tensor_scalar(conv_acc[:, c, :], src, w, pcol("conv_b", c), ALU.mult, ALU.add)
                else:
                    dve.wait_ge(conv_taps, n - 1)
                    ins = V.scalar_tensor_tensor(out=conv_acc[:, c, :], in0=src, scalar=w, in1=conv_acc[:, c, :],
                                                 op0=ALU.mult, op1=ALU.add)
                ins.then_inc(conv_taps, 1)

            def attend(u0, u1, gates_from=None, gate_tiles=()):
                for i in range(u0, u1 + 3):
                    g = None if gates_from is None else (i - gates_from - 1) // 4 - 1
                    if g is not None and g >= 0 and (i - gates_from - 1) % 4 == 0:
                        dve.wait_ge(*took(gate_tiles[g]))
                        link(V.tensor_scalar(sg[:, g, :], sg[:, g, :], 1.0, None, ALU.add))
                        link(V.reciprocal(sg[:, g, :], sg[:, g, :]))
                    if i < u1:
                        kind, h, t = units[i][:3]
                        w, mn = width(i), cols[:, 0, i % 64:i % 64 + 1]
                        dve.wait_ge(scored, i + 1)
                        if kind == "b1":
                            if i - 2 >= u0:
                                dve.wait_ge(row_exp, i - 1)
                            V.tensor_tensor_reduce(out=srow[:, i % 2, :], in0=ps[i % 3][:, :], in1=lnc[:, t, :], scale=1.0,
                                                   scalar=3e38, op0=ALU.add, op1=ALU.min, accum_out=mn).then_inc(row_min, 1)
                        else:
                            V.tensor_reduce(mn, ps[i % 3][:, 0:w], AX.X, ALU.min).then_inc(row_min, 1)
                        if u0 == 0:
                            conv_tap()
                            conv_tap()
                    j = i - 3
                    if j >= u0:
                        kind, h, t = units[j][:3]
                        k = j % 64
                        dve.wait_ge(row_exp, j + 1)
                        link(V.reciprocal(cols[:, 2, k:k + 1], cols[:, 1, k:k + 1]))
                        r, src = cols[:, 2, k:k + 1], ps[6 + j % 2][:, 0:HD]
                        if kind in ("sel", "win"):
                            link(V.tensor_tensor(cols[:, 3, k:k + 1], r, gates[:, t, 3 * h + (1 if kind == "sel" else 2):
                                                 3 * h + (2 if kind == "sel" else 3)], ALU.mult))
                        dve.wait_ge(pv_done, j + 1)
                        if kind in ("sel", "win"):
                            d = on[:, t, h * HD:(h + 1) * HD]
                            ins = V.scalar_tensor_tensor(out=d, in0=src, scalar=cols[:, 3, k:k + 1], in1=d,
                                                         op0=ALU.mult, op1=ALU.add)
                        else:
                            d = (o1[:, t, h * HD:(h + 1) * HD] if kind == "b1" else
                                 o1[:, t, 512 + h * HD:512 + (h + 1) * HD] if kind == "mem" else
                                 oa[:, t, h * HD:(h + 1) * HD])
                            ins = V.tensor_scalar(d, src, r, None, ALU.mult)
                        ins.then_inc(o_kept, 1)

            def keep_turned(n0, pairs):
                for n, (hi, lo) in enumerate(pairs):
                    dve.wait_ge(o_hi, n0 + n + 1)
                    V.tensor_tensor(lo, ps[4 + n % 2][:, :], hi.bitcast(f32), ALU.subtract).then_inc(o_lo, 1)

            def add_residual(ts_):
                for m, t in enumerate(ts_):
                    dve.wait_ge(blocks_done, filled(t))
                    V.tensor_tensor(x[:, m, :], ps[tiles[t][4]][:, :], x[:, m, :], ALU.add).then_inc(dve_took, 1)

            dve.wait_ge(par_loaded, 32)
            dve.wait_ge(pos_loaded, 16)
            V.tensor_scalar(neg_g[:, 0:1], pcol("q_g"), -1.0, None, ALU.mult)
            V.tensor_scalar(neg_g[:, 1:2], pcol("mq_g"), -1.0, None, ALU.mult)
            TWO_PI = 2 * np.pi
            C1 = 6.28125
            C2 = float(np.float32(np.round((TWO_PI - C1) * 2 ** 21) / 2 ** 21))
            C3 = TWO_PI - C1 - C2
            MAGIC = 12582912.0
            PI = 3.1415925
            ang, turns, red = (angle[:, i, :] for i in range(3))
            link(V.tensor_copy(pos_f[:, :], pos_i[:, :]))
            link(V.tensor_scalar(ang, pos_f[:, :], pcol("inv_freq"), None, ALU.mult))
            link(V.tensor_scalar(turns, ang, 1.0 / TWO_PI, MAGIC, ALU.mult, ALU.add))
            link(V.tensor_scalar(turns, turns, -MAGIC, None, ALU.add))
            for c_ in (C1, C2, C3):
                link(V.scalar_tensor_tensor(out=ang, in0=turns, scalar=-c_, in1=ang, op0=ALU.mult, op1=ALU.add))
            link(V.tensor_scalar(turns, ang, np.pi / 2, None, ALU.add))
            link(V.tensor_scalar(red, turns, PI, -TWO_PI, ALU.is_gt, ALU.mult))
            link(V.tensor_tensor(turns, turns, red, ALU.add))
            link(V.tensor_scalar(turns, turns, PI, -PI, ALU.min, ALU.max))
            V.tensor_scalar(ang, ang, PI, -PI, ALU.min, ALU.max).then_inc(trig_angle, 1)
            for n in range(4):
                dve.wait_ge(x_loaded[n], 16)
            norm(0, x, hn_hi, hn_lo)
            norm(1, mem_x, mn_hi, mn_lo, NMEM)
            V.memset(km[64:128, :, 0, :], 0.0)
            V.memset(km[0:64, :, 1, :], 0.0)
            V.memset(conv_in[:, :, 0:HALO], 0.0)
            V.memset(conv_in[:, :, HALO + S:], 0.0)
            dve.wait_ge(trig_ready, 2)
            V.memset(k1[64:128, :, 0, :], 0.0)
            link(V.memset(k1[0:64, :, 1, :], 0.0))
            normed, roped_n = [], 0
            for t in IN1:
                if tiles[t][0] in ("q", "k", "qm", "km"):
                    normed.append(t)
            rope_list = [t for t in normed if tiles[t][0] in ("q", "k")]
            for i in range(len(IN1) + 2):
                if i < len(IN1) and tiles[IN1[i]][0] == "gg":
                    dve.wait_ge(*took(IN1[i]))
                    c = tiles[IN1[i]][1]
                    V.tensor_tensor(conv_in[:, c, HALO:HALO + S], ps[tiles[IN1[i - 1]][4]][:, :], tmp[:, 2, :],
                                    ALU.mult).then_inc(dve_took, 1)
                if 0 <= i - 1 < len(IN1) and IN1[i - 1] in normed:
                    t = IN1[i - 1]
                    kind, idx, _, _, bank = tiles[t][:5]
                    w = NMEM if kind == "km" else S
                    e = normed.index(t)
                    dve.wait_ge(qk_rt, e + 1)
                    link(V.reciprocal(ri[:, 0:w], rt[:, 0:w]))
                    src = ps[bank]

                    def scaled(d, rows, g):
                        return V.scalar_tensor_tensor(out=d, in0=src[rows, 0:w], scalar=g, in1=ri[rows, 0:w],
                                                      op0=ALU.mult, op1=ALU.mult)
                    everyone = slice(0, P)
                    if kind == "q":
                        scaled(tmp[:, rope_list.index(t) % 2, :], everyone, neg_g[:, 0:1]).then_inc(dve_took, 1)
                    elif kind == "k":
                        scaled(tmp[:, rope_list.index(t) % 2, :], everyone, pcol("k_g")).then_inc(dve_took, 1)
                    elif kind == "qm":
                        scaled(qm[:, idx, :], everyone, neg_g[:, 1:2]).then_inc(dve_took, 1)
                    else:
                        g_ = PAR["mk_g"][0]
                        scaled(km[0:64, idx, 0, :], slice(0, 64), par[0:64, g_:g_ + 1])
                        scaled(km[64:128, idx, 1, :], slice(64, 128), par[64:128, g_:g_ + 1]).then_inc(dve_took, 1)
                if 0 <= i - 2 < len(IN1) and IN1[i - 2] in rope_list:
                    t = IN1[i - 2]
                    kind, idx = tiles[t][:2]
                    n = rope_list.index(t)
                    a_ = tmp[:, n % 2, :]
                    dve.wait_ge(*took(t))
                    if n:
                        dve.wait_ge(roped, n)
                    link(V.tensor_tensor(t1[:, :], a_, cos1[:, :], ALU.mult))
                    dve.wait_ge(rotated, n + 1)
                    link(V.tensor_tensor(a_, ps[5][:, :], sin1[:, :], ALU.mult))
                    if kind == "q":
                        V.tensor_tensor(q1[:, idx, :], t1[:, :], a_, ALU.add).then_inc(roped, 1)
                    else:
                        V.tensor_tensor(k1[0:64, idx, 0, :], t1[0:64, :], tmp[0:64, n % 2, :], ALU.add)
                        V.tensor_tensor(k1[64:128, idx, 1, :], t1[64:128, :], tmp[64:128, n % 2, :], ALU.add).then_inc(roped, 1)
            dve.wait_ge(lnc_loaded, 16)
            dve.wait_ge(dve_took, tiles[IN1[14]][6])
            attend(0, len(U1))
            while taps[0] < 2 * CONV_K:
                conv_tap()
            dve.wait_ge(ln_sum, 1)
            for c in range(2):
                V.tensor_tensor(conv_acc[:, c, :], conv_acc[:, c, :], ps[0][:, :], ALU.subtract).then_inc(ln_centred, 1)
            dve.wait_ge(ln_rt, 1)
            link(V.reciprocal(ri[:, :], rt[:, :]))
            for c in range(2):
                V.scalar_tensor_tensor(out=tmp[:, c, :], in0=conv_acc[:, c, :], scalar=pcol("ln_g", c), in1=ri[:, :],
                                       op0=ALU.mult, op1=ALU.mult).then_inc(ln_full, 1)
            keep_turned(0, [(mix_hi[:, c, :], mix_lo[:, c, :]) for c in (0, 1, 2, 3, 6, 7)])
            for c in range(2):
                dve.wait_ge(ln_hi, c + 1)
                V.tensor_tensor(mix_lo[:, 4 + c, :], tmp[:, c, :], mix_hi[:, 4 + c, :].bitcast(f32),
                                ALU.subtract).then_inc(ln_lo, 1)
            add_residual(OUT1)
            norm(2, x, hn_hi, hn_lo)
            for j in range(22):
                for k in range(2):
                    t = UP1[2 * j + k]
                    ch, y, src = j + 22 * k, yrow[:, (2 * j + k) % 4, :], ps[tiles[t][4]]
                    dve.wait_ge(ff_lin, 2 * j + k + 1)
                    link(V.scalar_tensor_tensor(out=y[:, 1:S], in0=src[:, 0:S - 1], scalar=pcol("ffn_w", 3 * ch),
                                                in1=y[:, 1:S], op0=ALU.mult, op1=ALU.add))
                    V.scalar_tensor_tensor(out=y[:, 0:S - 1], in0=src[:, 1:S], scalar=pcol("ffn_w", 3 * ch + 2),
                                           in1=y[:, 0:S - 1], op0=ALU.mult, op1=ALU.add).then_inc(dve_took, 1)
                dve.wait_ge(*took(UP1[2 * j + 1]))
                dve.wait_ge(ff_silu, j + 1)
                V.tensor_tensor(tmp[:, j % 3, :], yrow[:, (2 * j) % 4, :], yrow[:, (2 * j + 1) % 4, :],
                                ALU.mult).then_inc(ff_full, 1)
                dve.wait_ge(ff_full, j + 1)
                dve.wait_ge(ff_hi, j + 1)
                V.tensor_tensor(hid1_lo[:, j, :], tmp[:, j % 3, :], hid1_hi[:, j, :].bitcast(f32),
                                ALU.subtract).then_inc(ff_lo, 1)
            add_residual(DN1)

            roped_n, turned = 8, 6
            for l in range(LAYERS):
                ph = LIN[l]
                dve.wait_ge(blocks_done, B_L + l * LAYER_BLOCKS)
                V.memset(ka[64:128, :, 0, :], 0.0)
                V.memset(ka[0:64, :, 1, :], 0.0)
                V.memset(ksw[64:128, :, 0, :], 0.0)
                V.memset(ksw[0:64, :, 1, :], 0.0)
                V.memset(kc[:, :, :], 0.0)
                V.memset(vbd[:, :, :], 0.0)
                link(V.memset(c3[:, :], 0.0))
                norm(3 + 2 * l, x, hn_hi, hn_lo)
                jobs = ph["in"]
                dve.wait_ge(trig2_loaded, 16 * (l + 1))
                for i in range(len(jobs) + 2):
                    if i < len(jobs) and tiles[jobs[i]][0] == "cmp":
                        kv = tiles[jobs[i]][1]
                        dve.wait_ge(*took(jobs[i]))
                        for g in range(2):
                            src = cmp_t[:, g, 0:1]
                            src = bass.AP(src.tensor, src.offset, [src.ap[0], [2, 16], [CMP_STEP, NCMP]])
                            d = cmp_g[:, kv, 0:16 * 62].rearrange("p (j g n) -> p j g n", j=16, g=2)[:, :, g, :]
                            pv = pcol(f"pos_{'kv'[kv]}{l}", 0, 16)
                            pv = bass.AP(pv.tensor, pv.offset, [pv.ap[0], [1, 16], [0, NCMP]])
                            ins = V.tensor_tensor(d, src, pv, ALU.add)
                        ins.then_inc(cmp_full, 1)
                    if 0 <= i - 1 < len(jobs) and tiles[jobs[i - 1]][0] == "gate":
                        dve.wait_ge(fg_turned, l + 1)
                        z, za, ze = z32[:, 0, :, :], z32[:, 1, :, :], z32[:, 2, :, :]
                        w_, s_, s2, p_, mz = (s8[:, n, :, :] for n in range(5))
                        zin = ps[4][:, 0:P].rearrange("p (t n) -> p t n", t=TT)
                        link(V.tensor_copy(z, zin))
                        link(V.tensor_copy(za, z))
                        V.scalar_tensor_tensor(out=za[:, :, 0:8], in0=z[:, :, 0:8], scalar=-1.0, in1=z[:, :, 0:8],
                                               op0=ALU.mult, op1=ALU.max).then_inc(fg_abs, 1)
                        link(V.tensor_scalar(mz, z[:, :, 0:8], 0.0, None, ALU.min))
                        dve.wait_ge(fg_exp, l + 1)
                        link(V.tensor_scalar(gates[:, :, :], ze[:, :, 8:32], 1.0, None, ALU.add))
                        link(V.reciprocal(gates[:, :, :], gates[:, :, :]))
                        e8 = ze[:, :, 0:8]
                        link(V.tensor_scalar(w_, e8, 2.0, None, ALU.add))
                        link(V.reciprocal(w_, w_))
                        link(V.tensor_tensor(s_, e8, w_, ALU.mult))
                        link(V.tensor_tensor(s2, s_, s_, ALU.mult))
                        link(V.tensor_scalar(p_, s2, 1.0 / 17, None, ALU.mult))
                        for k in (15, 13, 11, 9, 7, 5, 3):
                            link(V.scalar_tensor_tensor(out=p_, in0=p_, scalar=1.0 / k, in1=s2, op0=ALU.add, op1=ALU.mult))
                        link(V.scalar_tensor_tensor(out=p_, in0=p_, scalar=1.0, in1=s_, op0=ALU.add, op1=ALU.mult))
                        V.scalar_tensor_tensor(out=lf[:, :, :], in0=p_, scalar=-2.0, in1=mz, op0=ALU.mult,
                                               op1=ALU.add).then_inc(fg_log, 1)
                    if 0 <= i - 2 < len(jobs) and tiles[jobs[i - 2]][0] == "gate":
                        dve.wait_ge(fg_cum, l + 1)
                        cum = ps[4][0:8, :]
                        link(V.tensor_copy(c3[0:8, :], cum))
                        link(V.tensor_tensor(rt[0:8, :], cum, c3[0:8, :], ALU.subtract))
                        link(V.tensor_copy(mid_b[0:8, :], rt[0:8, :]))
                        V.tensor_copy(c3[32:40, :], mid_b[0:8, :])
                        link(V.tensor_tensor(t1[0:8, :], rt[0:8, :], mid_b[0:8, :], ALU.subtract))
                        V.tensor_copy(c3[64:72, :], t1[0:8, :]).then_inc(fg_parts, 1)
                    if 0 <= i - 2 < len(jobs) and tiles[jobs[i - 2]][0] in ("qr", "kr"):
                        t = jobs[i - 2]
                        kind, idx = tiles[t][:2]
                        a_ = tmp[:, roped_n % 2, :]
                        dve.wait_ge(rotated, roped_n + 1)
                        dve.wait_ge(fg_parts, l + 1)
                        dve.wait_ge(roped, roped_n)
                        link(V.tensor_tensor(t1[:, :], a_, cs2[:, 0, :], ALU.mult))
                        link(V.tensor_tensor(a_, ps[5][:, :], cs2[:, 1, :], ALU.mult))
                        if kind == "qr":
                            V.tensor_tensor(qb[:, idx, :], t1[:, :], a_, ALU.add).then_inc(roped, 1)
                        else:
                            V.tensor_tensor(ksw[0:64, idx, 0, :], t1[0:64, :], tmp[0:64, roped_n % 2, :], ALU.add)
                            V.tensor_tensor(ksw[64:128, idx, 1, :], t1[64:128, :], tmp[64:128, roped_n % 2, :],
                                            ALU.add).then_inc(roped, 1)
                        roped_n += 1
                dve.wait_ge(roped, roped_n)
                dve.wait_ge(cmp_out, 2 * l + 1)
                V.tensor_scalar(t1[:, 0:62], ps[4][:, 0:62], pcol(f"b2_k{l}"), None, ALU.add).then_inc(cmp_biased, 1)
                dve.wait_ge(cmp_out, 2 * l + 2)
                a_ = PAR[f"b2_v{l}"][0]
                link(V.tensor_tensor(tmp[0:NCMP, 2, 0:P], ps[6][0:NCMP, 0:P], par[0:NCMP, a_:a_ + P], ALU.add))
                for r in range(4):
                    ins = V.tensor_copy(vbd[32 * r:32 * r + NCMP, :, r * HD:(r + 1) * HD],
                                        tmp[0:NCMP, 2, 0:P].rearrange("p (g d) -> p g d", g=2))
                ins.then_inc(cmp_kept, 1)
                dve.wait_ge(cmp_rot, l + 1)
                for g in range(2):
                    cs_ = [cs2[:, n, CMP_LEN - 1:CMP_LEN - 1 + CMP_STEP * (NCMP - 1) + 1:CMP_STEP] for n in range(2)]
                    sl = slice(g * NCMP, (g + 1) * NCMP)
                    link(V.tensor_tensor(tmp[:, 0, sl], t1[:, sl], cs_[0], ALU.mult))
                    link(V.tensor_tensor(tmp[:, 1, sl], ps[5][:, sl], cs_[1], ALU.mult))
                    rows = slice(64 * g, 64 * g + 64)
                    ins = V.tensor_tensor(kc[rows, g, :], tmp[rows, 0, sl], tmp[rows, 1, sl], ALU.add)
                ins.then_inc(cmp_kept, 1)
                link(V.memset(cprob[:, :, :, NCMP:32], 0.0))
                for t in range(TT):
                    dve.wait_ge(c_scored, TT * l + t + 1)
                    sc = ps[t][:, 0:8 * NCMP].rearrange("p (h n) -> p h n", h=8)
                    mn = cmpc[:, 0, t, :]
                    link(V.tensor_reduce(mn, sc, AX.X, ALU.min))
                    mnb = bass.AP(mn.tensor, mn.offset, [mn.ap[0], [1, 8], [0, NCMP]])
                    V.tensor_tensor(crow[:, t, 0:8 * NCMP].rearrange("p (h n) -> p h n", h=8), sc, mnb,
                                    ALU.subtract).then_inc(c_shift, 1)
                for t in range(TT):
                    dve.wait_ge(c_exp, TT * l + t + 1)
                    pr = cprob[:, t, :, 0:NCMP]
                    link(V.tensor_reduce(cmpc[:, 1, t, :], pr, AX.X, ALU.add))
                    if t == 0:
                        vb = bass.AP(valid0.tensor, valid0.offset, [valid0.ap[0], [0, 8], [1, NCMP]])
                        link(V.tensor_tensor(pr, pr, vb, ALU.mult))
                    link(V.reciprocal(cmpc[:, 2, t, :], cmpc[:, 1, t, :]))
                    V.tensor_tensor(cmpc[:, 3, t, :], cmpc[:, 2, t, :], gates[:, t, 0:22:3], ALU.mult).then_inc(c_prob, 1)
                for t in range(TT):
                    dve.wait_ge(c_pv, TT * l + t + 1)
                    w_ = cmpc[:, 3, t, :]
                    wb = bass.AP(w_.tensor, w_.offset, [w_.ap[0], [1, 8], [0, HD]])
                    V.tensor_tensor(on[:, t, :].rearrange("p (h d) -> p h d", h=8),
                                    ps[6 + t % 2][:, :].rearrange("p (h d) -> p h d", h=8), wb, ALU.mult).then_inc(c_o, 1)
                dve.wait_ge(c_o, TT * (l + 1))
                u1 = FIRST["nsa", l] + len(UN)
                attend(FIRST["fox", l], u1, FIRST["nsa", l], ph["gates"])
                keep_turned(turned, [(ya_hi[:, c, :], ya_lo[:, c, :]) for c in range(4)]
                            + [(yn_hi[:, c, :], yn_lo[:, c, :]) for c in range(4)])
                turned += 8
                for m in range(DC):
                    fox_, nsa_ = ph["mix"][m]
                    dve.wait_ge(blocks_done, filled(fox_))
                    if m:
                        dve.wait_ge(mix_full, DC * l + m)
                    V.tensor_tensor(mt[:, 0, :], ps[tiles[fox_][4]][:, :], sg[:, 2 * m, :], ALU.mult).then_inc(dve_took, 1)
                    V.tensor_tensor(mt[:, 1, :], ps[tiles[nsa_][4]][:, :], sg[:, 2 * m + 1, :], ALU.mult).then_inc(dve_took, 1)
                    dve.wait_ge(*took(nsa_))
                    V.tensor_tensor(tmp[:, m % 3, :], mt[:, 0, :], mt[:, 1, :], ALU.add).then_inc(mix_full, 1)
                    dve.wait_ge(mix_rounded, DC * l + m + 1)
                    V.tensor_tensor(mx_lo[:, m, :], tmp[:, m % 3, :], mx_hi[:, m, :].bitcast(f32),
                                    ALU.subtract).then_inc(mix_split, 1)
                add_residual(ph["out"])
                norm(4 + 2 * l, x, hn_hi, hn_lo)
                for half in range(2):
                    for i, t in enumerate(ph[f"up{half}"]):
                        n = 22 + 32 * l + 16 * half + i
                        dve.wait_ge(*took(t))
                        dve.wait_ge(ff_lo, n)
                        link(V.tensor_tensor(t1[:, :], tmp[:, n % 3, :], tmp[:, n % 3, :], ALU.mult))
                        dve.wait_ge(ff_hi, n + 1)
                        V.tensor_tensor(hid_lo[:, i, :], t1[:, :], hid_hi[:, i, :].bitcast(f32),
                                        ALU.subtract).then_inc(ff_lo, 1)
                    add_residual(ph[f"down{half}"])
            norm(7, x, None, None)


def _blocks(w, chunks=8):
    k, m = w.shape
    kc_, mt_ = k // P, m // P
    w = w.reshape(kc_, P, mt_, P).transpose(2, 1, 0, 3)
    pad = -kc_ % 8
    if pad:
        w = np.concatenate([w, np.zeros((mt_, P, pad, P), w.dtype)], axis=2)
    return w.reshape(mt_, P, (kc_ + pad) // 8, 1024).transpose(0, 2, 1, 3).reshape(-1, P, 1024)


def _stream(i):
    w = i["w_in"][0]
    out = [_blocks(w[:, :1536])]
    glu = w[:, 1536:2048].reshape(D, 2, 2, P).transpose(0, 2, 1, 3).reshape(D, 512)
    out += [_blocks(glu), _blocks(w[:, 2048:]), _blocks(i["w_mem_kv"][0]), _blocks(i["w_out"][0])]
    up = i["w_up"][0].reshape(D, 2, 22, P).transpose(0, 2, 1, 3).reshape(D, 2 * FF1)
    out += [_blocks(up), _blocks(i["w_down"][0])]
    for l in range(LAYERS):
        w = i["w_in_2"][l]
        cut = np.cumsum([512, 512, 512, 8, 512, 768, 24, D])
        q_a, k_a, v_a, f_a, q_b, kv_b, g_b, ga, gb = np.split(w, cut, axis=1)
        fg = np.concatenate([f_a, g_b, np.zeros((D, P - 32), w.dtype)], axis=1)
        q_b = q_b.reshape(D, 2, 4, HD).transpose(0, 2, 1, 3).reshape(D, 512)
        kv = kv_b.reshape(D, 6, P)
        out += [_blocks(a) for a in (kv[:, 0], kv[:, 1], fg, k_a)]
        w1 = [_blocks(a) for a in i["cmp_w1_2"][l]]
        w1 = [w1[0][:2], w1[0][2:], w1[1][:2], w1[1][2:]]
        tail = np.concatenate([kv[:, n] for n in (2, 4, 3, 5)], axis=1)
        for n, a in enumerate((q_a, v_a, q_b, tail)):
            out += [w1[n], _blocks(a)]
        out.append(np.stack([_blocks(ga), _blocks(gb)], axis=1).reshape(-1, P, 1024))
        out.append(_blocks(np.concatenate([i["w_o_fox_2"][l], i["w_o_nsa_2"][l]], axis=0)))
        out.append(_blocks(i["w_out_2"][l]))
        for half in range(2):
            a, b = half * 2048, (half + 1) * 2048
            out += [_blocks(i["w_up_2"][l][:, a:b]), _blocks(i["w_down_2"][l][a:b])]
    return np.ascontiguousarray(np.concatenate(out, axis=0))


def _params(i):
    f = np.float32
    par = np.zeros((P, NPAR), f)

    def put(name, a):
        at, w = PAR[name]
        par[:a.shape[0], at:at + w] = a

    def chunks(v):
        return v.reshape(-1, P).T
    put("mix_g", chunks(i["mix_norm_g"][0]))
    put("mem_g", chunks(i["mem_norm_g"][0]))
    put("ffn_g", chunks(i["ffn_norm_g"][0]))
    for name, key in (("q_g", "q_norm_g"), ("k_g", "k_norm_g"), ("mq_g", "mq_norm_g"), ("mk_g", "mk_norm_g")):
        put(name, np.concatenate([i[key][0]] * 2)[:, None])
    put("conv_w", i["conv_dw_w"][0].reshape(CONV_K, 2, P).transpose(2, 1, 0).reshape(P, -1))
    put("conv_b", chunks(i["conv_dw_b"][0]))
    put("ln_g", chunks(i["conv_ln_g"][0]))
    put("ln_b", chunks(i["conv_ln_b"][0]))
    put("ffn_w", i["ffn_dw_w"][0].reshape(3, 44, P).transpose(2, 1, 0).reshape(P, -1))
    put("ffn_b", chunks(i["ffn_dw_b"][0]))
    put("eps", np.full((P, 1), EPS, f))
    put("eps64", np.full((P, 1), 64 * EPS, f))
    put("norm_final", chunks(i["norm_final_2"]))
    inv = _inv_freq()
    a = np.zeros((P, 1), f)
    for h in (0, 64):
        a[h:h + 8, 0] = a[h + 8:h + 16, 0] = inv
    put("inv_freq", a)
    for l in range(LAYERS):
        put(f"norm_mix{l}", chunks(i["norm_mix_2"][l]))
        put(f"norm_mlp{l}", chunks(i["norm_mlp_2"][l]))
        put(f"fgate_b{l}", i["b_forget_2"][l][:, None])
        for n, kv in enumerate("kv"):
            put(f"pos_{kv}{l}", i["cmp_pos_2"][l][n].reshape(16, P).T)
            put(f"b1_{kv}{l}", chunks(i["cmp_b1_2"][l][n]))
        put(f"b2_k{l}", np.concatenate([i["cmp_b2_2"][l][0]] * 2)[:, None])
        put(f"b2_v{l}", np.broadcast_to(np.concatenate([i["cmp_b2_2"][l][1]] * 2), (P, P)))
        w2 = i["cmp_w2_2"][l].reshape(2, 2, P, HD)
        put(f"w2_k{l}", np.concatenate([w2[0], w2[0]], axis=2).transpose(1, 0, 2).reshape(P, -1))
        put(f"w2_v{l}", w2[1].transpose(1, 0, 2).reshape(P, -1))
    return par


def _inv_freq():
    f = np.float32
    return np.power(f(500000.0), -np.arange(0, 16, 2, dtype=f) / f(16)).astype(f)


def _constants():
    f = np.float32
    p = np.arange(P)
    rot = np.zeros((P, P), f)
    for h in (0, 64):
        for d in range(8):
            rot[h + d + 8, h + d] = -1.0
            rot[h + d, h + d + 8] = 1.0
    headmean = (p[:, None] // HD == p[None, :] // HD).astype(f) / HD
    tri = (np.arange(S)[None, :] >= p[:, None]).astype(f)
    end = np.arange(NCMP) * CMP_STEP + CMP_LEN - 1
    valid0 = np.zeros((P, 32), f)
    valid0[:, :NCMP] = end[None, :] <= p[:, None]
    fconst = np.concatenate([np.eye(P, dtype=f), rot, headmean, np.full((P, P), 1 / D, f),
                             np.full((P, P), 1 / CONV_W, f), tri, valid0], axis=1)
    causal = np.where(p[None, :] > p[:, None], f(BIG), f(0))
    q = np.arange(S).reshape(TT, P).T
    cmask = np.where(end[None, None, None, :] <= q[:, :, None, None], f(0), f(BIG))
    cmask = np.broadcast_to(cmask, (P, TT, 8, NCMP)).reshape(P, -1)
    sel = np.zeros((P, 8, P), f)
    for h in range(8):
        for part in (0, 32, 64):
            sel[part + h, h, :] = 1.0
    bconst = np.concatenate([np.eye(P, dtype=f), causal, cmask, sel.reshape(P, -1)], axis=1).astype(np.dtype("bfloat16"))
    i = np.arange(S)
    gap = np.abs(i[:, None] - i[None, :])
    count = (gap <= 64).astype(int) + ((gap % 4 == 0) & (gap <= 256)) + ((gap % 16 == 0) & (gap <= 1024))
    lnc = np.where(count > 0, -np.log(np.maximum(count, 1)), BIG).astype(f)
    lnc = lnc.reshape(TT, P, S).transpose(1, 0, 2)
    inv = np.zeros((P, 1), f)
    for h in (0, 64):
        inv[h:h + 8, 0] = inv[h + 8:h + 16, 0] = _inv_freq()
    ang = (i[None, :].astype(f) * inv).astype(f)
    trig2 = np.stack([np.cos(ang), np.sin(ang)], axis=1).astype(f)
    return fconst, bconst, np.ascontiguousarray(lnc), np.ascontiguousarray(trig2)


def kernel(**inputs):
    import concourse.bacc as bacc
    from concourse.bass_utils import run_bass_kernel_spmd

    i = {k: np.asarray(v) for k, v in inputs.items()}
    fconst, bconst, lnc, trig2 = _constants()
    arrays = {
        "xT": np.ascontiguousarray(i["x"][0].T.reshape(DC, P, S).transpose(1, 0, 2)),
        "memT": np.ascontiguousarray(i["mem"][0].T.reshape(DC, P, NMEM).transpose(1, 0, 2)),
        "positions": np.ascontiguousarray(i["positions"]),
        "wstream": _stream(i), "params": _params(i), "fconst": fconst, "bconst": bconst,
        "lncount": lnc, "trig2": trig2,
    }
    nc = bacc.Bacc("TRN2", target_bir_lowering=False, num_devices=1)
    aps = [nc.dram_tensor(n, a.shape, mybir.dt.from_np(a.dtype), kind="ExternalInput").ap() for n, a in arrays.items()]
    out = nc.dram_tensor("out", (P, DC, S), mybir.dt.float32, kind="ExternalOutput").ap()
    build(nc, *aps, out)
    got = run_bass_kernel_spmd(nc, [arrays], core_ids=[0]).results[0]["out"]
    return np.ascontiguousarray(got.transpose(1, 0, 2).reshape(D, S).T)[None]
```

```python
import numpy as np
import concourse.bass as bass
from concourse import mybir
from contextlib import ExitStack

P = 128
S = 512
D = 1024
DC = D // P
HD = 64
NMEM = 256
CONV_K, CONV_W = 31, 256
HALO = CONV_K // 2
FF1, FF2 = 2816, 4096
LAYERS = 2
CMP_LEN, CMP_STEP = 32, 16
NCMP = (S - CMP_LEN) // CMP_STEP + 1
EPS = 1e-6
BIG = 1e30
TT = S // P

RING = 3
B_IN1, B_OUT1, B_UP1, B_DOWN1 = 0, 22, 30, 74
DOWN1_BLOCKS = 3
B_L = B_DOWN1 + DC * DOWN1_BLOCKS
IN2, TURNS, GATES, BOTH, OUT2, UPDOWN = 0, 7, 31, 47, 55, 63
LAYER_BLOCKS = UPDOWN + 64
NBLOCKS = B_L + LAYERS * LAYER_BLOCKS

_PAR = [("mix_g", 8), ("mem_g", 8), ("ffn_g", 8), ("q_g", 1), ("k_g", 1), ("mq_g", 1), ("mk_g", 1),
        ("conv_w", 2 * CONV_K), ("conv_b", 2), ("ln_g", 2), ("ln_b", 2), ("ffn_w", 44 * 3),
        ("ffn_b", 44), ("inv_freq", 1), ("eps", 1), ("eps64", 1), ("norm_final", 8)]
for _l in range(LAYERS):
    _PAR += [(f"norm_mix{_l}", 8), (f"norm_mlp{_l}", 8), (f"fgate_b{_l}", 1), (f"pos_k{_l}", 16),
             (f"pos_v{_l}", 16), (f"b1_k{_l}", 2), (f"b1_v{_l}", 2), (f"b2_k{_l}", 1), (f"b2_v{_l}", P),
             (f"w2_k{_l}", 2 * P), (f"w2_v{_l}", P)]
PAR, _at = {}, 0
for _n, _w in _PAR:
    PAR[_n] = (_at, _w)
    _at += _w
NPAR = _at


def build(nc, xT, memT, positions, wstream, params, fconst, bconst, lncount, trig2, out):
    dt = mybir.dt
    f32, f32r, bf16 = dt.float32, dt.float32r, dt.bfloat16
    ALU, ACT, AX = mybir.AluOpType, mybir.ActivationFunctionType, mybir.AxisListType
    ctx = ExitStack()
    with ctx:
        KIB = 1024
        base = 16512

        def at(name, shape, dtype, offset):
            return nc.alloc_sbuf_tensor_at(name, [P, *shape], dtype, offset=base + offset)

        def sem(name):
            return ctx.enter_context(nc.semaphore(name))

        w_raw = at("w_raw", [RING, 1024], f32, 0)
        w_hi = at("w_hi", [RING, 1024], f32r, 12 * KIB)
        w_lo = at("w_lo", [RING, 1024], f32r, 24 * KIB)
        x = at("x", [DC, S], f32, 36 * KIB)
        hn_hi = at("hn_hi", [DC, S], f32r, 52 * KIB)
        hn_lo = at("hn_lo", [DC, S], f32r, 68 * KIB)
        R = 84 * KIB
        T = R + 88 * KIB
        q1 = at("q1", [4, S], f32, R)
        k1 = at("k1", [4, 2, S], f32, R + 8 * KIB)
        v1 = at("v1", [TT, 512], f32, R + 24 * KIB)
        qm = at("qm", [2, S], f32, R + 32 * KIB)
        km = at("km", [2, 2, NMEM], f32, R + 36 * KIB)
        vm = at("vm", [2, 256], f32, R + 40 * KIB)
        conv_in = at("conv_in", [2, S + 2 * HALO], f32, R + 42 * KIB)
        lnr = at("lnr", [S], f32, T + 12 * KIB)
        lni = at("lni", [S], f32, T + 14 * KIB)
        sqc = at("sqc", [2, S], f32, R + 63 * KIB)
        lny = at("lny", [2, S], f32, R + 83 * KIB)
        conv_acc = at("conv_acc", [2, S], f32, R + 47 * KIB)
        o1 = at("o1", [TT, 768], f32, R + 51 * KIB)
        lnc = at("lnc", [TT, S], f32, R + 67 * KIB)
        srow = at("srow", [2, S], f32, R + 75 * KIB)
        vt1 = at("vt1", [2, S], f32, R + 75 * KIB)
        cos1 = at("cos1", [S], f32, R + 79 * KIB)
        sin1 = at("sin1", [S], f32, R + 81 * KIB)
        mem_x = at("mem_x", [DC, NMEM], f32, R)
        mn_hi = at("mn_hi", [DC, NMEM], f32r, R + 51 * KIB)
        mn_lo = at("mn_lo", [DC, NMEM], f32r, R + 59 * KIB)
        angle = at("angle", [3, S], f32, R + 8 * KIB)
        pos_i = at("pos_i", [S], dt.int32, R + 14 * KIB)
        pos_f = at("pos_f", [S], f32, R + 16 * KIB)
        mix_hi = at("mix_hi", [DC, S], f32r, 52 * KIB)
        mix_lo = at("mix_lo", [DC, S], f32r, 68 * KIB)
        hid1_hi = at("hid1_hi", [22, S], f32r, R)
        hid1_lo = at("hid1_lo", [22, S], f32r, R + 44 * KIB)
        qa = at("qa", [4, S], f32, R)
        ka = at("ka", [4, 2, S], f32, R + 8 * KIB)
        va = at("va", [TT, 512], f32, R + 24 * KIB)
        qb = at("qb", [4, S], f32, R + 32 * KIB)
        ksw = at("ksw", [2, 2, S], f32, R + 40 * KIB)
        vsw = at("vsw", [2, TT, P], f32, R + 48 * KIB)
        kc = at("kc", [2, NCMP], f32, R + 52 * KIB)
        vbd = at("vbd", [2, 256], f32, R + 52 * KIB + 512)
        hidc = at("hidc", [2, 2, 62], f32, R + 54 * KIB + 512)
        gates = at("gates", [TT, 24], f32, R + 55 * KIB + 512)
        c3 = at("c3", [S], bf16, R + 56 * KIB)
        lf = at("lf", [TT, 8], f32, R + 57 * KIB)
        fgs = at("fgs", [S], f32, R + 57 * KIB + 128)
        z32 = at("z32", [3, TT, 32], f32, R + 59 * KIB + 256)
        s8 = at("s8", [5, TT, 8], f32, R + 60 * KIB + 896)
        oa = at("oa", [TT, 512], f32, R + 66 * KIB)
        on = at("on", [TT, 512], f32, R + 74 * KIB)
        cmp_t = at("cmp_t", [2, S], f32, R + 66 * KIB)
        cmp_g = at("cmp_g", [2, 1024], f32, R + 70 * KIB)
        cs2 = at("cs2", [2, S], f32, R + 82 * KIB)
        sg = at("sg", [2 * DC, S], f32, R)
        mx = at("mx", [DC, 2, S], f32r, R)
        mx_hi, mx_lo = mx[:, :, 0, :], mx[:, :, 1, :]
        ya_hi = at("ya_hi", [4, S], f32r, R + 32 * KIB)
        ya_lo = at("ya_lo", [4, S], f32r, R + 40 * KIB)
        yn_hi = at("yn_hi", [4, S], f32r, R + 48 * KIB)
        yn_lo = at("yn_lo", [4, S], f32r, R + 56 * KIB)
        mt = at("mt", [2, S], f32, R + 74 * KIB)
        hid_hi = at("hid_hi", [16, S], f32r, R)
        hid_lo = at("hid_lo", [16, S], f32r, R + 32 * KIB)
        sq = at("sq", [2, S], f32, T)
        rt = at("rt", [S], f32, T + 4 * KIB)
        ri = at("ri", [S], f32, T + 6 * KIB)
        tmp = at("tmp", [3, S], f32, T + 8 * KIB)
        t1 = at("t1", [S], f32, T + 14 * KIB)
        acc = t1
        mid_b = at("mid_b", [S], bf16, T + 6 * KIB)
        prow = at("prow", [3, S], f32, T)
        pT = at("pT", [3, S], f32, T + 6 * KIB)
        crow = at("crow", [256], f32, T + 12 * KIB)
        cprob = at("cprob", [8, 32], f32, T + 13 * KIB)
        cprobT = at("cprobT", [256], f32, T + 14 * KIB)
        yrow = at("yrow", [4, S], f32, T)
        yout = at("yout", [DC, S], f32, 52 * KIB)
        Q = T + 16 * KIB
        par = at("par", [NPAR], f32, Q)
        Q += (NPAR * 4 + 31) // 32 * 32
        fc = at("fc", [5 * P + S + 32], f32, Q)
        Q += (5 * P + S + 32) * 4
        bc = at("bc", [2 * P + 4 * 248 + 8 * P], bf16, Q)
        Q += (2 * P + 4 * 248 + 8 * P) * 2
        neg_g = at("neg_g", [2], f32, Q)
        zero = at("zero", [1], f32, Q + 32 + 1024 + 512)
        cols = at("cols", [4, 64], f32, Q + 32)
        cmpc = at("cmpc", [4, TT, 8], f32, Q + 32 + 1024)
        assert base + Q + 64 + 1024 + 512 <= nc.sbuf_usable_end
        ident, rot, headmean, mean1024, mean256 = (fc[:, i * P:(i + 1) * P] for i in range(5))
        tri = fc[:, 5 * P:5 * P + S]
        valid0 = fc[:, 5 * P + S:5 * P + S + NCMP]
        identb, causal = bc[:, 0:P], bc[:, P:2 * P]
        cmask = bc[:, 2 * P:2 * P + 4 * 248].rearrange("p (t n) -> p t n", t=4)
        headsel = bc[:, 2 * P + 4 * 248:].rearrange("p (h n) -> p h n", h=8)

        def pcol(name, i=0, n=1):
            a = PAR[name][0] + i
            return par[:, a:a + n]

        ps = [ctx.enter_context(nc.psum_tensor(f"bank{i}", [P, S], f32)) for i in range(8)]

        w_loaded = [sem(f"w_loaded{i}") for i in range(RING)]
        zero_set, w_rounded, w_split, blocks_done = sem("zero_set"), sem("w_rounded"), sem("w_split"), sem("blocks_done")
        x_loaded = [sem(f"x_loaded{n}") for n in range(4)]
        mem_loaded, par_loaded, mask_loaded, pos_loaded, lnc_loaded = (
            sem(n) for n in ("mem_loaded", "par_loaded", "mask_loaded", "pos_loaded", "lnc_loaded"))
        norm_sq, norm_sum, norm_rt, norm_full, norm_hi, norm_lo = (
            sem(n) for n in ("norm_sq", "norm_sum", "norm_rt", "norm_full", "norm_hi", "norm_lo"))
        norm_acc, norm_ri, norm_row = sem("norm_acc"), sem("norm_ri"), sem("norm_row")
        act_took, dve_took, dve_chain, act_chain = (
            sem(n) for n in ("act_took", "dve_took", "dve_chain", "act_chain"))
        qk_sq, qk_sum, qk_rt = sem("qk_sq"), sem("qk_sum"), sem("qk_rt")
        rotated, roped, v_turned, v_kept = sem("rotated"), sem("roped"), sem("v_turned"), sem("v_kept")
        trig_angle, trig_ready = sem("trig_angle"), sem("trig_ready")
        scored, row_min, row_exp, p_turned, p_kept, pv_done, o_kept = (
            sem(n) for n in ("scored", "row_min", "row_exp", "p_turned", "p_kept", "pv_done", "o_kept"))
        conv_taps, ln_sum, ln_centred, ln_sq, ln_rt, ln_full, ln_hi, ln_lo = (
            sem(n) for n in ("conv_taps", "ln_sum", "ln_centred", "ln_sq", "ln_rt", "ln_full", "ln_hi", "ln_lo"))
        o_turned, o_hi, o_lo = sem("o_turned"), sem("o_hi"), sem("o_lo")
        ff_lin, ff_silu, ff_full, ff_hi, ff_lo = (
            sem(n) for n in ("ff_lin", "ff_silu", "ff_full", "ff_hi", "ff_lo"))
        mix_full, mix_rounded, mix_split = sem("mix_full"), sem("mix_rounded"), sem("mix_split")
        fg_turned, fg_abs, fg_exp, fg_log, fg_cum, fg_parts = (
            sem(n) for n in ("fg_turned", "fg_abs", "fg_exp", "fg_log", "fg_cum", "fg_parts"))
        cmp_full, cmp_out, cmp_biased, cmp_rot, cmp_kept = (
            sem(n) for n in ("cmp_full", "cmp_out", "cmp_biased", "cmp_rot", "cmp_kept"))
        c_scored, c_shift, c_exp, c_prob, c_turned, c_kept, c_pv, c_o = (
            sem(n) for n in ("c_scored", "c_shift", "c_exp", "c_prob", "c_turned", "c_kept", "c_pv", "c_o"))
        trig2_loaded, out_full, out_stored = sem("trig2_loaded"), sem("out_full"), sem("out_stored")

        tiles, taken = [], {"act": 0, "dve": 0}
        TAKER = {"q": "dve", "k": "dve", "qm": "dve", "km": "dve", "v": "act", "vm": "act", "ga": "dve",
                 "gg": "act", "add": "dve", "fg": "dve", "fu": "dve", "cp": "act", "kz": "act",
                 "gate": "act", "qr": "act", "kr": "act", "cmp": "act", "w1": "act", "sig": "act",
                 "fox": "dve", "nsa": "dve", "relu": "act"}

        def tile(kind, i, block, n, bank=None):
            who = TAKER[kind]
            taken[who] += 1
            tiles.append((kind, i, block, n, len(tiles) % 4 if bank is None else bank, who, taken[who]))
            return len(tiles) - 1

        IN1 = []
        for kind, i in (("ga", 0), ("gg", 0), ("ga", 1), ("gg", 1), *(("q", c) for c in range(4)),
                        *(("k", c) for c in range(4)), ("qm", 0), ("qm", 1), ("km", 0), ("km", 1),
                        *(("v", c) for c in range(4)), ("vm", 0), ("vm", 1)):
            IN1.append(tile(kind, i, B_IN1 + len(IN1), 1))
        OUT1 = [tile("add", m, B_OUT1 + m, 1) for m in range(DC)]
        UP1 = [tile(("fg", "fu")[i % 2], i // 2, B_UP1 + i, 1) for i in range(44)]
        DN1 = [tile("add", m, B_DOWN1 + DOWN1_BLOCKS * m, DOWN1_BLOCKS) for m in range(DC)]
        HEAD2 = [("cmp", 0), ("cmp", 1), ("gate", 0)] + [("kz", i) for i in range(4)]
        TURN2 = [[("cp", i) for i in range(4)], [("v", i) for i in range(4)], [("qr", i) for i in range(4)],
                 [("kr", 0), ("kr", 1), ("v", 4), ("v", 5)]]
        LIN = []
        for l in range(LAYERS):
            o = B_L + l * LAYER_BLOCKS
            ph = {"in": [tile(k, i, o + IN2 + n, 1) for n, (k, i) in enumerate(HEAD2)]}
            for n, four in enumerate(TURN2):
                c = o + TURNS + 6 * n
                ph["in"].append(tile("w1", n, c, 2))
                ph["in"] += [tile(k, i, c + 2 + m, 1) for m, (k, i) in enumerate(four)]
            ph["cmp"] = [t for t in ph["in"] if tiles[t][0] == "w1"]
            ph["gates"] = [tile("sig", n, o + GATES + n, 1, 3) for n in range(16)]
            ph["mix"] = [[tile(k, m, o + BOTH + m, 1, 2 * (m % 3) + n) for n, k in enumerate(("fox", "nsa"))]
                         for m in range(DC)]
            ph["out"] = [tile("add", m, o + OUT2 + m, 1) for m in range(DC)]
            for half in range(2):
                u = o + UPDOWN + 32 * half
                ph[f"up{half}"] = [tile("relu", i, u + i, 1) for i in range(16)]
                ph[f"down{half}"] = [tile("add", m, u + 16 + 2 * m, 2) for m in range(DC)]
            LIN.append(ph)

        def filled(t):
            return tiles[t][2] + tiles[t][3]

        def took(t):
            return (act_took if tiles[t][5] == "act" else dve_took), tiles[t][6]

        NORM_AFTER = {2: OUT1, 3: DN1, 4: LIN[0]["out"], 5: LIN[0]["down1"], 6: LIN[1]["out"], 7: LIN[1]["down1"]}
        NORM_G = {0: "mix_g", 1: "mem_g", 2: "ffn_g", 3: "norm_mix0", 4: "norm_mlp0", 5: "norm_mix1",
                  6: "norm_mlp1", 7: "norm_final"}

        U1 = [("b1", h, t) for h in range(8) for t in range(TT)] + [("mem", h, t) for h in range(4) for t in range(TT)]
        UF = [("fox", h, t) for h in range(8) for t in range(TT)]
        UN = [(k, h, t) for k in ("sel", "win") for h in range(8) for t in range(TT)]
        units, FIRST = list(U1), {"b1": 0}
        for l in range(LAYERS):
            FIRST["fox", l] = len(units)
            units += [u + (l,) for u in UF]
            FIRST["nsa", l] = len(units)
            units += [u + (l,) for u in UN]
        NU = len(units)

        def width(u):
            kind, _, t = units[u][:3]
            return S if kind == "b1" else NMEM if kind == "mem" else P * (t + 1)

        def turn_bank(u1, c):
            return (u1 + c) % 3 if c < 3 else c

        LN_AT, TURN_AT = 33, (38, 40, 42, 44)
        LIN_OF = {FIRST["fox", l]: l for l in range(LAYERS)}
        RUNS = [(RING, B_L + TURNS), (B_L + TURNS + 24, B_L + LAYER_BLOCKS + TURNS),
                (B_L + LAYER_BLOCKS + TURNS + 24, NBLOCKS)]

        block = ctx.enter_context(nc.Block())

        @block.sync
        def _(sp):
            for n in range(4):
                sp.dma_start(x[:, 2 * n:2 * n + 2, :], xT[:, 2 * n:2 * n + 2, :]).then_inc(x_loaded[n], 16)
            for s in range(RING):
                sp.dma_start(w_raw[:, s, :], wstream[s]).then_inc(w_loaded[s], 16)
            sp.dma_start(mem_x[:, :, :], memT).then_inc(mem_loaded, 16)

            def load(slot, b, unsplit_before=False):
                if unsplit_before:
                    sp.wait_ge(blocks_done, b + (1 - RING))
                else:
                    sp.wait_ge(w_split, b + (1 - RING))
                sp.dma_start(w_raw[:, slot, :], wstream[b]).then_inc(w_loaded[slot], 16)

            for b0, b1 in RUNS:
                with sp.Fori(0, (b1 - b0) // RING) as turn:
                    for j in range(RING):
                        load((b0 + j) % RING, turn * RING + (b0 + j))
                for b in range(b0 + (b1 - b0) // RING * RING, b1):
                    load(b % RING, b)
                if b1 < NBLOCKS:
                    with sp.Fori(0, 4) as turn:
                        for j in range(6):
                            load((b1 + j) % RING, turn * 6 + (b1 + j), unsplit_before=j in (3, 4))

        @block.gpsimd
        def _(pool):
            def split(slot, loads, b, first=False):
                pool.wait_ge(w_loaded[slot], loads * 16)
                if not first:
                    pool.wait_ge(blocks_done, b + (1 - RING))
                nc.gpsimd.tensor_tensor(w_hi[:, slot, :], w_raw[:, slot, :], zeros,
                                        ALU.add).then_inc(w_rounded, 1)
                pool.wait_ge(w_rounded, b + 1)
                nc.gpsimd.tensor_tensor(w_lo[:, slot, :], w_raw[:, slot, :], w_hi[:, slot, :].bitcast(f32),
                                        ALU.subtract).then_inc(w_split, 1)

            nc.gpsimd.memset(zero[:, :], 0.0).then_inc(zero_set, 1)
            zeros = bass.AP(zero[:, :].tensor, zero[:, :].offset, [zero[:, :].ap[0], [0, 1024]])
            pool.wait_ge(zero_set, 1)
            for s in range(RING):
                split(s, 1, s, first=True)
            for b0, b1 in RUNS:
                with pool.Fori(0, (b1 - b0) // RING) as turn:
                    for j in range(RING):
                        split((b0 + j) % RING, turn + ((b0 + j) // RING + 1), turn * RING + (b0 + j))
                for b in range(b0 + (b1 - b0) // RING * RING, b1):
                    split(b % RING, b // RING + 1, b)
                if b1 < NBLOCKS:
                    with pool.Fori(0, 4) as turn:
                        for j in range(6):
                            slot, loads = (b1 + j) % RING, turn * 2 + ((b1 + j) // RING + 1)
                            if j < 2:
                                pool.wait_ge(w_loaded[slot], loads * 16)
                                pool.wait_ge(w_split, turn * 6 + (b1 + j))
                                pool.sem_inc(w_rounded, 1)
                                pool.sem_inc(w_split, 1)
                            else:
                                split(slot, loads, turn * 6 + (b1 + j))

        @block.tensor
        def _(pe):
            last_on_bank = {}

            def linear(t, hi, lo, cols_, chunks, ready=None, first_chunk=0, last=True, base=0, part=None):
                kind, i, block_, n, bank, _, _ = tiles[t]
                c0, c1 = part or (0, chunks)
                if c0 == 0:
                    if bank in last_on_bank:
                        pe.wait_ge(*took(last_on_bank[bank]))
                    last_on_bank[bank] = t
                for c in range(c0, c1):
                    b_, j = block_ + (c + base) // 8, (c + base) % 8
                    if j == 0 or c == 0:
                        pe.wait_ge(w_split, b_ + 1)
                    if ready is not None:
                        pe.wait_ge(ready[0], ready[1] + c + 1)
                    wh, wl = w_hi[:, b_ % RING, j * P:(j + 1) * P], w_lo[:, b_ % RING, j * P:(j + 1) * P]
                    a_h, a_l = hi[:, first_chunk + c, 0:cols_], lo[:, first_chunk + c, 0:cols_]
                    nc.tensor.matmul(ps[bank][:, 0:cols_], wh, a_h, start=c == 0, stop=False)
                    nc.tensor.matmul(ps[bank][:, 0:cols_], wh, a_l, start=False, stop=False)
                    mm = nc.tensor.matmul(ps[bank][:, 0:cols_], wl, a_h, start=False, stop=c == chunks - 1)
                    if last and (j == 7 or c == chunks - 1):
                        mm.then_inc(blocks_done, 1)

            def linear_w1(t):
                kind, n, block_, _, bank, _, _ = tiles[t]
                pe.wait_ge(*took(last_on_bank[bank]))
                last_on_bank[bank] = t
                for c in range(16):
                    b_, j = block_ + c // 8, c % 8
                    if j == 0:
                        pe.wait_ge(w_split, b_ + 1)
                    mm = nc.tensor.matmul(ps[bank][:, 0:2 * NCMP], w_raw[:, b_ % RING, j * P:(j + 1) * P],
                                          cmp_g[:, n // 2, c * 2 * NCMP:(c + 1) * 2 * NCMP], start=c == 0, stop=c == 15)
                    if j == 7:
                        mm.then_inc(blocks_done, 1)

            def norm_mean(n, cols_=S):
                last = (DC - 1) % 2
                for part in range(2):
                    if part == 0:
                        pe.wait_ge(norm_acc, (DC - 2) * (n + 1))
                        if n:
                            pe.wait_ge(norm_full, DC * n)
                    else:
                        pe.wait_ge(norm_sq, DC * (n + 1))
                    src = sq[:, last, :] if part else acc[:, :]
                    for t in range(cols_ // P):
                        mm = nc.tensor.matmul(ps[7][:, t:t + 1], src[:, t * P:(t + 1) * P], mean1024[:, 0:1],
                                              start=part == t == 0, stop=part == 1 and t == cols_ // P - 1)
                mm.then_inc(norm_sum, 1)

            def norm_spread(n, cols_=S):
                pe.wait_ge(norm_ri, n + 1)
                for t in range(cols_ // P):
                    col = ri[:, t:t + 1]
                    mm = nc.tensor.matmul(ps[7][:, t * P:(t + 1) * P], bass.AP(col.tensor, col.offset, [col.ap[0], [0, P]]),
                                          ident, start=True, stop=True)
                mm.then_inc(norm_row, 1)

            def norm(n):
                norm_mean(n)
                norm_spread(n)

            def linear_pair(ta, tb, ready):
                for c in range(DC):
                    linear(ta, hn_hi, hn_lo, S, DC, ready, part=(c, c + 1))
                    linear(tb, hn_hi, hn_lo, S, DC, part=(c, c + 1))

            def turn_tile(src, bank, n, rows=P):
                for t in range(n):
                    mm = nc.tensor.transpose(ps[bank][:, t * rows:(t + 1) * rows], src[0:rows, t * P:(t + 1) * P],
                                             ident[0:rows, 0:rows])
                return mm

            def rotate(n, src, cols_=S):
                if n:
                    pe.wait_ge(roped, n)
                nc.tensor.matmul(ps[5][:, 0:cols_], rot, src, start=True, stop=True).then_inc(rotated, 1)

            def turn_out(src, bank):
                for t in range(TT):
                    mm = nc.tensor.transpose(ps[bank][:, t * P:(t + 1) * P], src[:, t, :], ident)
                mm.then_inc(o_turned, 1)

            def attend(u0, u1, gates_from=None, gate_tiles=()):
                for i in range(u0, u1 + 4):
                    if i < u1:
                        kind, h, t = units[i][:3]
                        bank, w = ps[i % 3], width(i)
                        if kind == "b1":
                            q_, k_ = q1[:, h // 2, t * P:(t + 1) * P], k1[:, h // 2, h % 2, :]
                        elif kind == "mem":
                            q_, k_ = qm[:, h // 2, t * P:(t + 1) * P], km[:, h // 2, h % 2, :]
                        elif kind == "fox":
                            q_, k_ = qa[:, h // 2, t * P:(t + 1) * P], ka[:, h // 2, h % 2, 0:w]
                        else:
                            q_ = qb[:, h % 4, t * P:(t + 1) * P]
                            k_ = ksw[:, 0 if kind == "sel" else 1, h // 4, 0:w]
                        plain = kind in ("b1", "mem")
                        mm = nc.tensor.matmul(bank[:, 0:w], q_, k_, start=True, stop=plain)
                        if kind == "fox":
                            nc.tensor.matmul(bank[:, 0:w], headsel[0:96, h, :], c3[0:96, 0:w], start=False, stop=False)
                        if not plain:
                            mm = nc.tensor.matmul(bank[:, t * P:w], identb, causal, start=False, stop=True)
                        mm.then_inc(scored, 1)
                    j = i - 2
                    if u0 <= j < u1:
                        pe.wait_ge(row_exp, j + 1)
                        for c in range(width(j) // P):
                            mm = nc.tensor.transpose(ps[4 + j % 2 * 1][:, c * P:(c + 1) * P],
                                                     prow[:, j % 3, c * P:(c + 1) * P], ident)
                        mm.then_inc(p_turned, 1)
                    j = i - 4
                    if j >= u0:
                        kind, h, t = units[j][:3]
                        n = width(j) // P
                        if i >= u1:
                            pe.wait_ge(p_kept, j + 1)
                        if j >= 2 and j - 2 >= u0:
                            pe.wait_ge(o_kept, j - 1)
                        for c in range(n):
                            if kind == "b1":
                                v_ = v1[:, c, h * HD:(h + 1) * HD]
                            elif kind == "mem":
                                v_ = vm[:, c, h * HD:(h + 1) * HD]
                            elif kind == "fox":
                                v_ = va[:, c, h * HD:(h + 1) * HD]
                            else:
                                v_ = vsw[:, 0 if kind == "sel" else 1, c, h // 4 * HD:(h // 4 + 1) * HD]
                            mm = nc.tensor.matmul(ps[6 + j % 2][:, 0:HD], pT[:, j % 3, c * P:(c + 1) * P], v_,
                                                  start=c == 0, stop=c == n - 1)
                        mm.then_inc(pv_done, 1)
                    if u0 == 0:
                        between1(i)
                    elif i < gates_from:
                        compressed(u0, i - u0)
                    if gates_from is not None and gates_from <= i < u1:
                        n = 2 * (i - gates_from)
                        if n == 0:
                            pe.wait_ge(c_o, TT * (LIN_OF[u0] + 1))
                        linear(gate_tiles[n // 8], hn_hi, hn_lo, S, DC, part=(n % 8, n % 8 + 2))
                    if gates_from is not None and i >= u1:
                        c = i - u1
                        if c == 3:
                            pe.wait_ge(*took(gate_tiles[-1]))
                        turn_out(oa[:, :, c * P:(c + 1) * P], turn_bank(u1, c))

            def between1(i):
                if i == LN_AT:
                    pe.wait_ge(conv_taps, 2 * CONV_K)
                    for c in range(2):
                        mm = nc.tensor.matmul(ps[3][:, :], mean256, conv_acc[:, c, :], start=c == 0, stop=c == 1)
                    mm.then_inc(ln_sum, 1)
                if i == LN_AT + 2:
                    pe.wait_ge(ln_centred, 2)
                    for c in range(2):
                        pe.wait_ge(ln_sq, c + 1)
                        mm = nc.tensor.matmul(ps[3][:, :], mean256, sqc[:, c, :], start=c == 0, stop=c == 1)
                    mm.then_inc(ln_sum, 1)
                if i in TURN_AT:
                    c = TURN_AT.index(i)
                    if c == 0:
                        pe.wait_ge(ln_rt, 1)
                        pe.wait_ge(o_kept, 32)
                    else:
                        pe.wait_ge(o_lo, c)
                    for t in range(TT):
                        mm = nc.tensor.transpose(ps[3][:, t * P:(t + 1) * P], o1[:, t, c * P:(c + 1) * P], ident)
                    mm.then_inc(o_turned, 1)

            def compressed(u0, n):
                t, step = n // 8, n % 8
                done = TT * LIN_OF[u0] + t
                if step == 1:
                    if t == 0:
                        pe.wait_ge(cmp_kept, 2 * (LIN_OF[u0] + 1))
                        pe.wait_ge(*took(last_on_bank[3]))
                    else:
                        pe.wait_ge(c_o, done)
                    nc.tensor.matmul(ps[3][:, 0:8 * NCMP], identb, cmask[:, t, :], start=True, stop=False)
                    for slot in range(8):
                        mm = nc.tensor.matmul(ps[3][:, slot * NCMP:(slot + 1) * NCMP], qb[:, slot % 4, t * P:(t + 1) * P],
                                              kc[:, slot // 4, :], start=False, stop=slot == 7)
                    mm.then_inc(c_scored, 1)
                if step == 4:
                    pe.wait_ge(c_prob, done + 1)
                    for g in range(2):
                        mm = nc.tensor.transpose(ps[3][:, g * P:(g + 1) * P],
                                                 cprob[:, 4 * g:4 * g + 4, :].rearrange("p a b -> p (a b)"), ident)
                    mm.then_inc(c_turned, 1)
                if step == 6:
                    pe.wait_ge(c_kept, done + 1)
                    for g in range(2):
                        mm = nc.tensor.matmul(ps[3][:, g * 256:(g + 1) * 256], cprobT[:, g * P:(g + 1) * P],
                                              vbd[:, g, :], start=True, stop=True)
                    mm.then_inc(c_pv, 1)

            def turn_outputs(n0, sources):
                for n, src in enumerate(sources):
                    k = n0 + n
                    if n >= 2:
                        pe.wait_ge(o_lo, k - 1)
                    for t in range(TT):
                        mm = nc.tensor.transpose(ps[4 + n % 2][:, t * P:(t + 1) * P], src[:, t, :], ident)
                    mm.then_inc(o_turned, 1)

            pe.wait_ge(par_loaded, 32)
            norm(0)
            qk, rope_n, v_n = {}, {}, {}
            for t in IN1:
                k = tiles[t][0]
                if k in ("q", "k", "qm", "km"):
                    qk[t] = len(qk)
                if k in ("q", "k"):
                    rope_n[t] = len(rope_n)
                if k in ("v", "vm"):
                    v_n[t] = len(v_n)
            for i in range(len(IN1) + 2):
                if i < len(IN1):
                    t = IN1[i]
                    if tiles[t][0] in ("km", "vm"):
                        linear(t, mn_hi, mn_lo, NMEM, DC, (norm_lo, DC) if tiles[t][:2] == ("km", 0) else None)
                    elif i == 0:
                        linear_pair(t, IN1[1], (norm_lo, 0))
                        norm_mean(1, NMEM)
                    elif i == 2:
                        linear(t, hn_hi, hn_lo, S, DC, part=(0, 2))
                        norm_spread(1, NMEM)
                        linear(t, hn_hi, hn_lo, S, DC, part=(2, DC))
                    elif i > 2:
                        linear(t, hn_hi, hn_lo, S, DC)
                if 0 <= i - 1 < len(IN1):
                    t = IN1[i - 1]
                    kind, w = tiles[t][0], NMEM if tiles[t][0] in ("km", "vm") else S
                    if t in qk:
                        pe.wait_ge(qk_sq, qk[t] + 1)
                        if qk[t]:
                            pe.wait_ge(qk_rt, qk[t])
                        nc.tensor.matmul(ps[4][:, 0:w], headmean, sq[:, qk[t] % 2, 0:w], start=True,
                                         stop=True).then_inc(qk_sum, 1)
                    if t in v_n:
                        pe.wait_ge(*took(t))
                        if v_n[t]:
                            pe.wait_ge(v_kept, v_n[t])
                        turn_tile(vt1[:, v_n[t] % 2, :], 6, w // P).then_inc(v_turned, 1)
                if 0 <= i - 2 < len(IN1) and IN1[i - 2] in rope_n:
                    t = IN1[i - 2]
                    pe.wait_ge(*took(t))
                    rotate(rope_n[t], tmp[:, rope_n[t] % 2, :])
            pe.wait_ge(dve_took, tiles[IN1[15]][6])
            pe.wait_ge(act_took, tiles[IN1[-1]][6])
            pe.wait_ge(v_kept, len(v_n))
            pe.wait_ge(roped, len(rope_n))
            attend(0, len(U1))
            pe.wait_ge(p_kept, len(U1))
            pe.wait_ge(o_kept, len(U1))
            turn_outputs(4, [o1[:, :, c * P:(c + 1) * P] for c in (4, 5)])
            pe.wait_ge(o_lo, 4)
            linear(OUT1[0], mix_hi, mix_lo, S, DC, part=(0, 4))
            pe.wait_ge(ln_lo, 2)
            pe.wait_ge(o_lo, 6)
            linear(OUT1[0], mix_hi, mix_lo, S, DC, part=(4, DC))
            for t in OUT1[1:]:
                linear(t, mix_hi, mix_lo, S, DC)
            norm(2)
            linear_pair(UP1[0], UP1[1], (norm_lo, 2 * DC))
            for t in UP1[2:]:
                linear(t, hn_hi, hn_lo, S, DC)
            for n, t in enumerate(DN1):
                linear(t, hid1_hi, hid1_lo, S, 22, (ff_lo, 0) if n == 0 else None)

            roped_n, v_done, turned = len(rope_n), len(v_n), 6
            for l in range(LAYERS):
                ph = LIN[l]
                norm(3 + 2 * l)
                jobs = ph["in"]
                nrot = nv = 0
                for i in range(len(jobs) + 2):
                    if i == 0:
                        pe.wait_ge(mask_loaded, 16)
                    if i < len(jobs) and tiles[jobs[i]][0] == "w1":
                        if tiles[jobs[i]][1] % 2 == 0:
                            pe.wait_ge(cmp_full, 2 * l + tiles[jobs[i]][1] // 2 + 1)
                        linear_w1(jobs[i])
                    elif i == 0:
                        linear_pair(jobs[0], jobs[1], (norm_lo, DC * (3 + 2 * l)))
                    elif 1 < i < len(jobs):
                        linear(jobs[i], hn_hi, hn_lo, S, DC)
                    if 0 <= i - 1 < len(jobs):
                        t = jobs[i - 1]
                        kind = tiles[t][0]
                        if kind in ("qr", "kr"):
                            pe.wait_ge(*took(t))
                            rotate(roped_n, tmp[:, roped_n % 2, :])
                            roped_n += 1
                        if kind == "v":
                            pe.wait_ge(*took(t))
                            pe.wait_ge(v_kept, v_done)
                            turn_tile(sq[:, v_done % 2, :], 6, TT).then_inc(v_turned, 1)
                            v_done += 1
                        if kind == "gate":
                            pe.wait_ge(*took(t))
                            turn_tile(fgs[:, :], 4, TT, 32).then_inc(fg_turned, 1)
                    if 0 <= i - 2 < len(jobs) and tiles[jobs[i - 2]][0] == "gate":
                        pe.wait_ge(fg_log, l + 1)
                        for t in range(TT):
                            mm = nc.tensor.matmul(ps[4][0:8, t * P:S], lf[:, t, :], tri[:, 0:S - t * P],
                                                  start=t == 0, stop=t == TT - 1)
                        mm.then_inc(fg_cum, 1)
                pe.wait_ge(*took(ph["cmp"][1]))
                pe.wait_ge(fg_parts, l + 1)
                for g in range(2):
                    for f in range(2):
                        mm = nc.tensor.matmul(ps[4][:, g * NCMP:(g + 1) * NCMP], pcol(f"w2_k{l}", f * P, P),
                                              hidc[:, 0, f, g * NCMP:(g + 1) * NCMP], start=f == 0, stop=f == 1)
                mm.then_inc(cmp_out, 1)
                pe.wait_ge(*took(ph["cmp"][3]))
                pe.wait_ge(v_kept, v_done)
                for g in range(2):
                    for f in range(2):
                        mm = nc.tensor.matmul(ps[6][0:NCMP, g * HD:(g + 1) * HD], hidc[:, 1, f, g * NCMP:(g + 1) * NCMP],
                                              pcol(f"w2_v{l}", f * HD, HD), start=f == 0, stop=f == 1)
                mm.then_inc(cmp_out, 1)
                pe.wait_ge(cmp_biased, l + 1)
                pe.wait_ge(roped, roped_n)
                nc.tensor.matmul(ps[5][:, 0:2 * NCMP], rot, t1[:, 0:2 * NCMP], start=True,
                                 stop=True).then_inc(cmp_rot, 1)
                for n in (0, 1, 2):
                    pe.wait_ge(*took(last_on_bank[n]))
                pe.wait_ge(cmp_kept, 2 * (l + 1))
                pe.wait_ge(v_kept, v_done)
                u0, u1 = FIRST["fox", l], FIRST["nsa", l] + len(UN)
                attend(u0, u1, FIRST["nsa", l], ph["gates"])
                pe.wait_ge(o_kept, u1)
                for c in range(4):
                    turn_out(on[:, :, c * P:(c + 1) * P], 4 + c)
                turned += 8
                for m in range(DC):
                    fox_, nsa_ = ph["mix"][m]
                    if m == 0:
                        pe.wait_ge(o_lo, turned - 4)
                    linear(fox_, ya_hi, ya_lo, S, 4, last=False)
                    if m == 0:
                        pe.wait_ge(o_lo, turned)
                    linear(nsa_, yn_hi, yn_lo, S, 4, base=4)
                for n, t in enumerate(ph["out"]):
                    linear(t, mx_hi, mx_lo, S, DC, (mix_split, DC * l) if n == 0 else None)
                norm(4 + 2 * l)
                for half in range(2):
                    up = ph[f"up{half}"]
                    if half == 0:
                        linear_pair(up[0], up[1], (norm_lo, DC * (4 + 2 * l)))
                    for t in up[2 * (1 - half):]:
                        linear(t, hn_hi, hn_lo, S, DC)
                    for n, t in enumerate(ph[f"down{half}"]):
                        linear(t, hid_hi, hid_lo, S, 16, (ff_lo, 22 + 32 * l + 16 * half) if n == 0 else None)
            norm(7)

        @block.scalar
        def _(act):
            A = nc.scalar.activation
            act.dma_start(par[:, :], params).then_inc(par_loaded, 16)
            act.dma_start(fc[:, :], fconst).then_inc(par_loaded, 16)
            act.dma_start(pos_i[:, :], positions.to_broadcast([P, S])).then_inc(pos_loaded, 16)

            def norm(n, src, hi, cols_=S):
                for c in range(DC):
                    if n == 0 and c % 2 == 0:
                        act.wait_ge(x_loaded[c // 2], 16)
                    if n in NORM_AFTER:
                        act.wait_ge(dve_took, tiles[NORM_AFTER[n][c]][6])
                    if c >= 2:
                        act.wait_ge(norm_acc, (DC - 2) * n + max(c - 2, 1))
                    elif n:
                        act.wait_ge(norm_sum, n)
                    A(sq[:, c % 2, 0:cols_], src[:, c, :], ACT.Square).then_inc(norm_sq, 1)
                act.wait_ge(norm_sum, n + 1)
                if n == 0:
                    act.wait_ge(par_loaded, 32)
                A(rt[:, 0:cols_ // P], ps[7][:, 0:cols_ // P], ACT.Sqrt, bias=pcol("eps")).then_inc(norm_rt, 1)
                if hi is None:
                    return
                for c in range(DC):
                    act.wait_ge(norm_full, DC * n + c + 1)
                    A(hi[:, c, :], tmp[:, c % 3, 0:cols_], ACT.Copy).then_inc(norm_hi, 1)

            def attend(u0, u1, gates_from=None, gate_tiles=()):
                for i in range(u0, u1 + 2):
                    if u0 == 0:
                        between1(i)
                    elif i < gates_from:
                        compressed(u0, i - u0)
                    g = None if gates_from is None else (i - gates_from) // 4 - 1
                    if g is not None and g >= 0 and (i - gates_from) % 4 == 0:
                        t = gate_tiles[g]
                        act.wait_ge(blocks_done, filled(t))
                        if g == 0:
                            act.wait_ge(pv_done, gates_from)
                        A(sg[:, g, :], ps[3][:, :], ACT.Exp, scale=-1.0).then_inc(act_took, 1)
                    j = i - 2
                    if j >= u0:
                        w = width(j)
                        act.wait_ge(p_turned, j + 1)
                        A(pT[:, j % 3, 0:w], ps[4 + j % 2][:, 0:w], ACT.Copy).then_inc(p_kept, 1)
                    if i < u1:
                        kind, w = units[i][0], width(i)
                        act.wait_ge(row_min, i + 1)
                        src = srow[:, i % 2, :] if kind == "b1" else ps[i % 3][:, 0:w]
                        A(prow[:, i % 3, 0:w], src, ACT.Exp, scale=-1.0, bias=cols[:, 0, i % 64:i % 64 + 1],
                          accum_out=cols[:, 1, i % 64:i % 64 + 1]).then_inc(row_exp, 1)

            def between1(i):
                if i == LN_AT + 2:
                    for c in range(2):
                        act.wait_ge(ln_centred, c + 1)
                        A(sqc[:, c, :], conv_acc[:, c, :], ACT.Square).then_inc(ln_sq, 1)
                if i == LN_AT + 4:
                    act.wait_ge(ln_sum, 2)
                    A(lnr[:, :], ps[3][:, :], ACT.Sqrt, bias=pcol("eps")).then_inc(ln_rt, 1)
                if i - 1 in TURN_AT:
                    c = TURN_AT.index(i - 1)
                    act.wait_ge(o_turned, c + 1)
                    A(mix_hi[:, c, :], ps[3][:, :], ACT.Copy).then_inc(o_hi, 1)

            def compressed(u0, n):
                t, step = n // 8, n % 8
                done = TT * LIN_OF[u0] + t
                if step == 3:
                    act.wait_ge(c_shift, done + 1)
                    if t:
                        act.wait_ge(c_turned, done)
                    A(cprob[:, :, 0:NCMP], crow[:, 0:8 * NCMP].rearrange("p (h n) -> p h n", h=8), ACT.Exp,
                      scale=-1.0).then_inc(c_exp, 1)
                if step == 5:
                    act.wait_ge(c_turned, done + 1)
                    if t:
                        act.wait_ge(c_pv, done)
                    A(cprobT[:, :], ps[3][:, 0:256], ACT.Copy).then_inc(c_kept, 1)

            def keep_turned(n0, dests, banks):
                for n, d in enumerate(dests):
                    act.wait_ge(o_turned, n0 + n + 1)
                    A(d, ps[banks[n]][:, :], ACT.Copy).then_inc(o_hi, 1)

            norm(0, x, hn_hi)
            act.dma_start(lnc[:, :, :], lncount).then_inc(lnc_loaded, 16)
            act.dma_start(bc[:, :], bconst).then_inc(mask_loaded, 16)
            act.wait_ge(mem_loaded, 16)
            norm(1, mem_x, mn_hi, NMEM)
            act.wait_ge(trig_angle, 1)
            A(sin1[:, :], angle[:, 0, :], ACT.Sin).then_inc(trig_ready, 1)
            A(cos1[:, :], angle[:, 1, :], ACT.Sin).then_inc(trig_ready, 1)
            e_of, v_of, e, v = {}, {}, 0, 0
            for t in IN1:
                if tiles[t][0] in ("q", "k", "qm", "km"):
                    e_of[t] = e; e += 1
                if tiles[t][0] in ("v", "vm"):
                    v_of[t] = v; v += 1
            last_normed = None
            for i in range(len(IN1) + 1):
                if i < len(IN1):
                    t = IN1[i]
                    kind, _, _, _, bank = tiles[t][:5]
                    w = NMEM if kind in ("km", "vm") else S
                    act.wait_ge(blocks_done, filled(t))
                    if t in e_of:
                        if e_of[t] >= 2:
                            act.wait_ge(qk_sum, e_of[t] - 1)
                        A(sq[:, e_of[t] % 2, 0:w], ps[bank][:, 0:w], ACT.Square).then_inc(qk_sq, 1)
                    elif t in v_of:
                        if v_of[t] >= 2:
                            act.wait_ge(v_turned, v_of[t] - 1)
                        A(vt1[:, v_of[t] % 2, 0:w], ps[bank][:, 0:w], ACT.Copy).then_inc(act_took, 1)
                    elif kind == "gg":
                        if tiles[t][1]:
                            act.wait_ge(*took(IN1[i - 3]))
                        A(tmp[:, 2, :], ps[bank][:, :], ACT.Sigmoid).then_inc(act_took, 1)
                if i >= 1:
                    t = IN1[i - 1]
                    kind, idx = tiles[t][:2]
                    w = NMEM if kind in ("km", "vm") else S
                    if t in e_of:
                        act.wait_ge(qk_sum, e_of[t] + 1)
                        if last_normed is not None:
                            act.wait_ge(*took(last_normed))
                        last_normed = t
                        q_like = kind in ("q", "qm")
                        A(rt[:, 0:w], ps[4][:, 0:w], ACT.Sqrt, scale=64.0 if q_like else 1.0,
                          bias=pcol("eps64" if q_like else "eps")).then_inc(qk_rt, 1)
                    if t in v_of:
                        act.wait_ge(v_turned, v_of[t] + 1)
                        d = (v1[:, :, idx * P:(idx + 1) * P] if kind == "v" else vm[:, :, idx * P:(idx + 1) * P])
                        A(d, ps[6][:, 0:w].rearrange("p (t n) -> p t n", n=P), ACT.Copy).then_inc(v_kept, 1)
            attend(0, len(U1))
            for c in range(2):
                act.wait_ge(ln_full, c + 1)
                A(lny[:, c, :], lny[:, c, :], ACT.Silu, bias=pcol("ln_b", c)).then_inc(act_chain, 1)
                act.wait_ge(act_chain, c + 1)
                A(mix_hi[:, 4 + c, :], lny[:, c, :], ACT.Copy).then_inc(ln_hi, 1)
            keep_turned(4, [mix_hi[:, c, :] for c in (6, 7)], (4, 5))
            norm(2, x, hn_hi)
            for j in range(22):
                for k in range(2):
                    t = UP1[2 * j + k]
                    ch = j + 22 * k
                    act.wait_ge(blocks_done, filled(t))
                    if j >= 2:
                        act.wait_ge(ff_full, j - 1)
                    A(yrow[:, (2 * j + k) % 4, :], ps[tiles[t][4]][:, :], ACT.Identity, scale=pcol("ffn_w", 3 * ch + 1),
                      bias=pcol("ffn_b", ch)).then_inc(ff_lin, 1)
                act.wait_ge(*took(UP1[2 * j]))
                A(yrow[:, (2 * j) % 4, :], yrow[:, (2 * j) % 4, :], ACT.Silu).then_inc(ff_silu, 1)
                act.wait_ge(ff_full, j + 1)
                A(hid1_hi[:, j, :], tmp[:, j % 3, :], ACT.Copy).then_inc(ff_hi, 1)

            roped_n, v_done, turned = 8, 6, 6
            for l in range(LAYERS):
                ph = LIN[l]
                norm(3 + 2 * l, x, hn_hi)
                act.wait_ge(blocks_done, B_L + l * LAYER_BLOCKS)
                act.dma_start(cs2[:, :, :], trig2).then_inc(trig2_loaded, 16)
                jobs = ph["in"]
                for i in range(len(jobs) + 1):
                    if i < len(jobs):
                        t = jobs[i]
                        kind, idx, _, _, bank = tiles[t][:5]
                        act.wait_ge(blocks_done, filled(t))
                        src = ps[bank]
                        if kind == "w1":
                            A(hidc[:, idx // 2, idx % 2, :], src[:, 0:2 * NCMP], ACT.Gelu_apprx_tanh,
                              bias=pcol(f"b1_{'kv'[idx // 2]}{l}", idx % 2)).then_inc(act_took, 1)
                        elif kind == "cp":
                            A(qa[:, idx, :], src[:, :], ACT.Copy, scale=-0.125).then_inc(act_took, 1)
                        elif kind == "kz":
                            A(ka[0:64, idx, 0, :], src[0:64, :], ACT.Copy)
                            A(ka[64:128, idx, 1, :], src[64:128, :], ACT.Copy).then_inc(act_took, 1)
                        elif kind == "v":
                            vi = v_done + idx
                            act.wait_ge(v_turned, vi - 1)
                            A(sq[:, vi % 2, :], src[:, :], ACT.Copy).then_inc(act_took, 1)
                        elif kind == "gate":
                            A(fgs[0:32, :], src[0:32, :], ACT.Identity, bias=par[0:32, PAR[f"fgate_b{l}"][0]:PAR[f"fgate_b{l}"][0] + 1]).then_inc(act_took, 1)
                        elif kind in ("qr", "kr"):
                            rn = roped_n + idx + (4 if kind == "kr" else 0)
                            act.wait_ge(roped, rn - 1)
                            A(tmp[:, rn % 2, :], src[:, :], ACT.Copy,
                              scale=-0.125 if kind == "qr" else 1.0).then_inc(act_took, 1)
                        elif kind == "cmp":
                            if idx:
                                act.wait_ge(cmp_full, 2 * l + 1)
                            for g in range(2):
                                A(cmp_t[0:64, g, :], src[64 * g:64 * g + 64, :], ACT.Copy)
                                ins = A(cmp_t[64:128, g, 0:S - 1], src[64 * g:64 * g + 64, 1:S], ACT.Copy)
                            ins.then_inc(act_took, 1)
                    if i >= 1:
                        t = jobs[i - 1]
                        kind, idx = tiles[t][:2]
                        if kind == "v":
                            vi = v_done + idx
                            act.wait_ge(v_turned, vi + 1)
                            d = va[:, :, idx * P:(idx + 1) * P] if idx < 4 else vsw[:, idx - 4, :, :]
                            A(d, ps[6][:, :].rearrange("p (t n) -> p t n", n=P), ACT.Copy).then_inc(v_kept, 1)
                        if kind == "gate":
                            act.wait_ge(fg_abs, l + 1)
                            A(z32[:, 2, :, :], z32[:, 1, :, :], ACT.Exp, scale=-1.0).then_inc(fg_exp, 1)
                roped_n += 6
                v_done += 6
                attend(FIRST["fox", l], FIRST["nsa", l] + len(UN), FIRST["nsa", l], ph["gates"])
                u1 = FIRST["nsa", l] + len(UN)
                keep_turned(turned, [ya_hi[:, c, :] for c in range(4)] + [yn_hi[:, c, :] for c in range(4)],
                            [turn_bank(u1, c) for c in range(8)])
                turned += 8
                for m in range(DC):
                    act.wait_ge(mix_full, DC * l + m + 1)
                    A(mx_hi[:, m, :], tmp[:, m % 3, :], ACT.Copy).then_inc(mix_rounded, 1)
                norm(4 + 2 * l, x, hn_hi)
                for half in range(2):
                    for i, t in enumerate(ph[f"up{half}"]):
                        n = 22 + 32 * l + 16 * half + i
                        act.wait_ge(blocks_done, filled(t))
                        act.wait_ge(ff_lo, n - 2)
                        if half and i == 0:
                            act.wait_ge(blocks_done, filled(ph["down0"][-1]))
                        A(tmp[:, n % 3, :], ps[tiles[t][4]][:, :], ACT.Relu).then_inc(act_took, 1)
                        act.wait_ge(*took(t))
                        A(hid_hi[:, i, :], tmp[:, n % 3, :], ACT.Square).then_inc(ff_hi, 1)
            norm(7, x, None)
            for c in range(DC):
                act.wait_ge(out_full, c + 1)
                act.dma_start(out[:, c, :], yout[:, c, :]).then_inc(out_stored, 16)
            act.wait_ge(out_stored, 16 * DC)

        @block.vector
        def _(dve):
            V = nc.vector
            chain = [0]

            def link(ins):
                chain[0] += 1
                ins.then_inc(dve_chain, 1)
                dve.wait_ge(dve_chain, chain[0])

            def norm_add(n, c, cols_=S):
                dve.wait_ge(norm_sq, DC * n + c + 1)
                if c > 1:
                    dve.wait_ge(norm_acc, (DC - 2) * n + c - 1)
                V.tensor_tensor(acc[:, 0:cols_], sq[:, 0, 0:cols_] if c == 1 else acc[:, 0:cols_],
                                sq[:, c % 2, 0:cols_], ALU.add).then_inc(norm_acc, 1)

            def norm(n, src, hi, lo, cols_=S):
                dve.wait_ge(norm_rt, n + 1)
                V.reciprocal(ri[:, 0:cols_ // P], rt[:, 0:cols_ // P]).then_inc(norm_ri, 1)
                dve.wait_ge(norm_row, n + 1)
                for c in range(DC + 1):
                    if c < DC:
                        if c >= 3 and hi is not None:
                            dve.wait_ge(norm_lo, DC * n + c - 2)
                        d = tmp[:, c % 3, 0:cols_] if hi is not None else yout[:, c, :]
                        V.scalar_tensor_tensor(out=d, in0=src[:, c, :], scalar=pcol(NORM_G[n], c), in1=ps[7][:, 0:cols_],
                                               op0=ALU.mult, op1=ALU.mult).then_inc(norm_full if hi is not None else out_full, 1)
                    if c and hi is not None:
                        dve.wait_ge(norm_full, DC * n + c)
                        dve.wait_ge(norm_hi, DC * n + c)
                        V.tensor_tensor(lo[:, c - 1, :], tmp[:, (c - 1) % 3, 0:cols_], hi[:, c - 1, :].bitcast(f32),
                                        ALU.subtract).then_inc(norm_lo, 1)

            taps = [0]

            def conv_tap():
                n = taps[0]
                if n == 2 * CONV_K:
                    return
                taps[0] += 1
                c, k = n % 2, n // 2
                src, w = conv_in[:, c, k:k + S], pcol("conv_w", c * CONV_K + k)
                if k == 0:
                    ins = V.tensor_scalar(conv_acc[:, c, :], src, w, pcol("conv_b", c), ALU.mult, ALU.add)
                else:
                    dve.wait_ge(conv_taps, n - 1)
                    ins = V.scalar_tensor_tensor(out=conv_acc[:, c, :], in0=src, scalar=w, in1=conv_acc[:, c, :],
                                                 op0=ALU.mult, op1=ALU.add)
                ins.then_inc(conv_taps, 1)

            def between1(i):
                if i < LN_AT:
                    conv_tap()
                if i == LN_AT + 1:
                    dve.wait_ge(ln_sum, 1)
                    for c in range(2):
                        V.tensor_tensor(conv_acc[:, c, :], conv_acc[:, c, :], ps[3][:, :], ALU.subtract).then_inc(ln_centred, 1)
                if i == LN_AT + 4:
                    dve.wait_ge(ln_rt, 1)
                    link(V.reciprocal(lni[:, :], lnr[:, :]))
                    for c in range(2):
                        V.scalar_tensor_tensor(out=lny[:, c, :], in0=conv_acc[:, c, :], scalar=pcol("ln_g", c),
                                               in1=lni[:, :], op0=ALU.mult, op1=ALU.mult).then_inc(ln_full, 1)
                if i - 1 in TURN_AT:
                    c = TURN_AT.index(i - 1)
                    dve.wait_ge(o_hi, c + 1)
                    V.tensor_tensor(mix_lo[:, c, :], ps[3][:, :], mix_hi[:, c, :].bitcast(f32),
                                    ALU.subtract).then_inc(o_lo, 1)

            def compressed(u0, n):
                t, step = n // 8, n % 8
                done = TT * LIN_OF[u0] + t
                if step == 1:
                    dve.wait_ge(c_scored, done + 1)
                    sc = ps[3][:, 0:8 * NCMP].rearrange("p (h n) -> p h n", h=8)
                    mn = cmpc[:, 0, t, :]
                    link(V.tensor_reduce(mn, sc, AX.X, ALU.min))
                    mnb = bass.AP(mn.tensor, mn.offset, [mn.ap[0], [1, 8], [0, NCMP]])
                    V.tensor_tensor(crow[:, 0:8 * NCMP].rearrange("p (h n) -> p h n", h=8), sc, mnb,
                                    ALU.subtract).then_inc(c_shift, 1)
                if step == 3:
                    dve.wait_ge(c_exp, done + 1)
                    pr = cprob[:, :, 0:NCMP]
                    link(V.tensor_reduce(cmpc[:, 1, t, :], pr, AX.X, ALU.add))
                    if t == 0:
                        vb = bass.AP(valid0.tensor, valid0.offset, [valid0.ap[0], [0, 8], [1, NCMP]])
                        link(V.tensor_tensor(pr, pr, vb, ALU.mult))
                    link(V.reciprocal(cmpc[:, 2, t, :], cmpc[:, 1, t, :]))
                    V.tensor_tensor(cmpc[:, 3, t, :], cmpc[:, 2, t, :], gates[:, t, 0:22:3], ALU.mult).then_inc(c_prob, 1)
                if step == 7:
                    dve.wait_ge(c_pv, done + 1)
                    w_ = cmpc[:, 3, t, :]
                    wb = bass.AP(w_.tensor, w_.offset, [w_.ap[0], [1, 8], [0, HD]])
                    V.tensor_tensor(on[:, t, :].rearrange("p (h d) -> p h d", h=8),
                                    ps[3][:, :].rearrange("p (h d) -> p h d", h=8), wb, ALU.mult).then_inc(c_o, 1)

            def attend(u0, u1, gates_from=None, gate_tiles=()):
                for i in range(u0, u1 + 4):
                    g = None if gates_from is None else (i - gates_from - 1) // 4 - 1
                    if g is not None and 0 <= g < len(gate_tiles) - 1:
                        quarter = (i - gates_from - 1) % 4
                        if quarter == 0:
                            dve.wait_ge(*took(gate_tiles[g]))
                            link(V.tensor_scalar(sg[:, g, :], sg[:, g, :], 1.0, None, ALU.add))
                        part = slice(quarter * P, (quarter + 1) * P)
                        link(V.reciprocal(sg[:, g, part], sg[:, g, part]))
                    if i < u1:
                        kind, h, t = units[i][:3]
                        w, mn = width(i), cols[:, 0, i % 64:i % 64 + 1]
                        dve.wait_ge(scored, i + 1)
                        if kind == "b1":
                            if i - 2 >= u0:
                                dve.wait_ge(row_exp, i - 1)
                            V.tensor_tensor_reduce(out=srow[:, i % 2, :], in0=ps[i % 3][:, :], in1=lnc[:, t, :], scale=1.0,
                                                   scalar=3e38, op0=ALU.add, op1=ALU.min, accum_out=mn).then_inc(row_min, 1)
                        else:
                            V.tensor_reduce(mn, ps[i % 3][:, 0:w], AX.X, ALU.min).then_inc(row_min, 1)
                    if u0 == 0:
                        between1(i)
                    elif i < gates_from:
                        compressed(u0, i - u0)
                    j = i - 4
                    if j >= u0:
                        kind, h, t = units[j][:3]
                        k = j % 64
                        if i >= u1:
                            dve.wait_ge(row_exp, j + 1)
                        link(V.reciprocal(cols[:, 2, k:k + 1], cols[:, 1, k:k + 1]))
                        r, src = cols[:, 2, k:k + 1], ps[6 + j % 2][:, 0:HD]
                        if kind in ("sel", "win"):
                            link(V.tensor_tensor(cols[:, 3, k:k + 1], r, gates[:, t, 3 * h + (1 if kind == "sel" else 2):
                                                 3 * h + (2 if kind == "sel" else 3)], ALU.mult))
                        dve.wait_ge(pv_done, j + 1)
                        if kind in ("sel", "win"):
                            d = on[:, t, h * HD:(h + 1) * HD]
                            ins = V.scalar_tensor_tensor(out=d, in0=src, scalar=cols[:, 3, k:k + 1], in1=d,
                                                         op0=ALU.mult, op1=ALU.add)
                        else:
                            d = (o1[:, t, h * HD:(h + 1) * HD] if kind == "b1" else
                                 o1[:, t, 512 + h * HD:512 + (h + 1) * HD] if kind == "mem" else
                                 oa[:, t, h * HD:(h + 1) * HD])
                            ins = V.tensor_scalar(d, src, r, None, ALU.mult)
                        ins.then_inc(o_kept, 1)

            def keep_turned(n0, pairs, banks):
                for n, (hi, lo) in enumerate(pairs):
                    dve.wait_ge(o_hi, n0 + n + 1)
                    V.tensor_tensor(lo, ps[banks[n]][:, :], hi.bitcast(f32), ALU.subtract).then_inc(o_lo, 1)

            def add_residual(ts_, n=None):
                for m, t in enumerate(ts_):
                    dve.wait_ge(blocks_done, filled(t))
                    V.tensor_tensor(x[:, m, :], ps[tiles[t][4]][:, :], x[:, m, :], ALU.add).then_inc(dve_took, 1)
                    if n is not None and m >= 2:
                        norm_add(n, m - 1)

            for c in range(1, DC - 1):
                norm_add(0, c)
            dve.wait_ge(par_loaded, 32)
            dve.wait_ge(pos_loaded, 16)
            V.tensor_scalar(neg_g[:, 0:1], pcol("q_g"), -1.0, None, ALU.mult)
            V.tensor_scalar(neg_g[:, 1:2], pcol("mq_g"), -1.0, None, ALU.mult)
            TWO_PI = 2 * np.pi
            C1 = 6.28125
            C2 = float(np.float32(np.round((TWO_PI - C1) * 2 ** 21) / 2 ** 21))
            C3 = TWO_PI - C1 - C2
            MAGIC = 12582912.0
            PI = 3.1415925
            ang, turns, red = (angle[:, i, :] for i in range(3))
            link(V.tensor_copy(pos_f[:, :], pos_i[:, :]))
            link(V.tensor_scalar(ang, pos_f[:, :], pcol("inv_freq"), None, ALU.mult))
            link(V.tensor_scalar(turns, ang, 1.0 / TWO_PI, MAGIC, ALU.mult, ALU.add))
            link(V.tensor_scalar(turns, turns, -MAGIC, None, ALU.add))
            for c_ in (C1, C2, C3):
                link(V.scalar_tensor_tensor(out=ang, in0=turns, scalar=-c_, in1=ang, op0=ALU.mult, op1=ALU.add))
            for n in range(4):
                dve.wait_ge(x_loaded[n], 16)
            norm(0, x, hn_hi, hn_lo)
            link(V.tensor_scalar(turns, ang, np.pi / 2, None, ALU.add))
            link(V.tensor_scalar(red, turns, PI, -TWO_PI, ALU.is_gt, ALU.mult))
            link(V.tensor_tensor(turns, turns, red, ALU.add))
            link(V.tensor_scalar(turns, turns, PI, -PI, ALU.min, ALU.max))
            V.tensor_scalar(ang, ang, PI, -PI, ALU.min, ALU.max).then_inc(trig_angle, 1)
            for c in range(1, DC - 1):
                norm_add(1, c, NMEM)
            norm(1, mem_x, mn_hi, mn_lo, NMEM)
            V.memset(km[64:128, :, 0, :], 0.0)
            V.memset(km[0:64, :, 1, :], 0.0)
            V.memset(conv_in[:, :, 0:HALO], 0.0)
            V.memset(conv_in[:, :, HALO + S:], 0.0)
            normed, roped_n = [], 0
            for t in IN1:
                if tiles[t][0] in ("q", "k", "qm", "km"):
                    normed.append(t)
            rope_list = [t for t in normed if tiles[t][0] in ("q", "k")]
            for i in range(len(IN1) + 2):
                if i == 3:
                    dve.wait_ge(trig_ready, 2)
                    V.memset(k1[64:128, :, 0, :], 0.0)
                    link(V.memset(k1[0:64, :, 1, :], 0.0))
                if i < len(IN1) and tiles[IN1[i]][0] == "gg":
                    dve.wait_ge(*took(IN1[i]))
                    c = tiles[IN1[i]][1]
                    V.tensor_tensor(conv_in[:, c, HALO:HALO + S], ps[tiles[IN1[i - 1]][4]][:, :], tmp[:, 2, :],
                                    ALU.mult).then_inc(dve_took, 1)
                if 18 <= i < 24:
                    for _ in range(6):
                        conv_tap()
                if 0 <= i - 1 < len(IN1) and IN1[i - 1] in normed:
                    t = IN1[i - 1]
                    kind, idx, _, _, bank = tiles[t][:5]
                    w = NMEM if kind == "km" else S
                    e = normed.index(t)
                    dve.wait_ge(qk_rt, e + 1)
                    link(V.reciprocal(ri[:, 0:w], rt[:, 0:w]))
                    src = ps[bank]

                    def scaled(d, rows, g):
                        return V.scalar_tensor_tensor(out=d, in0=src[rows, 0:w], scalar=g, in1=ri[rows, 0:w],
                                                      op0=ALU.mult, op1=ALU.mult)
                    everyone = slice(0, P)
                    if kind == "q":
                        scaled(tmp[:, rope_list.index(t) % 2, :], everyone, neg_g[:, 0:1]).then_inc(dve_took, 1)
                    elif kind == "k":
                        scaled(tmp[:, rope_list.index(t) % 2, :], everyone, pcol("k_g")).then_inc(dve_took, 1)
                    elif kind == "qm":
                        scaled(qm[:, idx, :], everyone, neg_g[:, 1:2]).then_inc(dve_took, 1)
                    else:
                        g_ = PAR["mk_g"][0]
                        scaled(km[0:64, idx, 0, :], slice(0, 64), par[0:64, g_:g_ + 1])
                        scaled(km[64:128, idx, 1, :], slice(64, 128), par[64:128, g_:g_ + 1]).then_inc(dve_took, 1)
                if 0 <= i - 2 < len(IN1) and IN1[i - 2] in rope_list:
                    t = IN1[i - 2]
                    kind, idx = tiles[t][:2]
                    n = rope_list.index(t)
                    a_ = tmp[:, n % 2, :]
                    dve.wait_ge(*took(t))
                    if n:
                        dve.wait_ge(roped, n)
                    link(V.tensor_tensor(t1[:, :], a_, cos1[:, :], ALU.mult))
                    dve.wait_ge(rotated, n + 1)
                    link(V.tensor_tensor(a_, ps[5][:, :], sin1[:, :], ALU.mult))
                    if kind == "q":
                        V.tensor_tensor(q1[:, idx, :], t1[:, :], a_, ALU.add).then_inc(roped, 1)
                    else:
                        V.tensor_tensor(k1[0:64, idx, 0, :], t1[0:64, :], tmp[0:64, n % 2, :], ALU.add)
                        V.tensor_tensor(k1[64:128, idx, 1, :], t1[64:128, :], tmp[64:128, n % 2, :], ALU.add).then_inc(roped, 1)
            dve.wait_ge(lnc_loaded, 16)
            attend(0, len(U1))
            for c in range(2):
                dve.wait_ge(ln_hi, c + 1)
                V.tensor_tensor(mix_lo[:, 4 + c, :], lny[:, c, :], mix_hi[:, 4 + c, :].bitcast(f32),
                                ALU.subtract).then_inc(ln_lo, 1)
            keep_turned(4, [(mix_hi[:, c, :], mix_lo[:, c, :]) for c in (6, 7)], (4, 5))
            add_residual(OUT1, 2)
            norm(2, x, hn_hi, hn_lo)
            for j in range(22):
                for k in range(2):
                    t = UP1[2 * j + k]
                    ch, y, src = j + 22 * k, yrow[:, (2 * j + k) % 4, :], ps[tiles[t][4]]
                    dve.wait_ge(ff_lin, 2 * j + k + 1)
                    link(V.scalar_tensor_tensor(out=y[:, 1:S], in0=src[:, 0:S - 1], scalar=pcol("ffn_w", 3 * ch),
                                                in1=y[:, 1:S], op0=ALU.mult, op1=ALU.add))
                    V.scalar_tensor_tensor(out=y[:, 0:S - 1], in0=src[:, 1:S], scalar=pcol("ffn_w", 3 * ch + 2),
                                           in1=y[:, 0:S - 1], op0=ALU.mult, op1=ALU.add).then_inc(dve_took, 1)
                dve.wait_ge(*took(UP1[2 * j + 1]))
                dve.wait_ge(ff_silu, j + 1)
                V.tensor_tensor(tmp[:, j % 3, :], yrow[:, (2 * j) % 4, :], yrow[:, (2 * j + 1) % 4, :],
                                ALU.mult).then_inc(ff_full, 1)
                dve.wait_ge(ff_full, j + 1)
                dve.wait_ge(ff_hi, j + 1)
                V.tensor_tensor(hid1_lo[:, j, :], tmp[:, j % 3, :], hid1_hi[:, j, :].bitcast(f32),
                                ALU.subtract).then_inc(ff_lo, 1)
            add_residual(DN1, 3)

            roped_n, turned = 8, 6
            for l in range(LAYERS):
                ph = LIN[l]
                norm(3 + 2 * l, x, hn_hi, hn_lo)
                dve.wait_ge(blocks_done, B_L + l * LAYER_BLOCKS)
                V.memset(ka[64:128, :, 0, :], 0.0)
                V.memset(ka[0:64, :, 1, :], 0.0)
                V.memset(ksw[64:128, :, 0, :], 0.0)
                V.memset(ksw[0:64, :, 1, :], 0.0)
                V.memset(kc[:, :, :], 0.0)
                V.memset(vbd[:, :, :], 0.0)
                link(V.memset(c3[:, :], 0.0))
                jobs = ph["in"]
                dve.wait_ge(trig2_loaded, 16 * (l + 1))
                for i in range(len(jobs) + 2):
                    if i < len(jobs) and tiles[jobs[i]][0] == "cmp":
                        kv = tiles[jobs[i]][1]
                        dve.wait_ge(*took(jobs[i]))
                        for g in range(2):
                            src = cmp_t[:, g, 0:1]
                            src = bass.AP(src.tensor, src.offset, [src.ap[0], [2, 16], [CMP_STEP, NCMP]])
                            d = cmp_g[:, kv, 0:16 * 62].rearrange("p (j g n) -> p j g n", j=16, g=2)[:, :, g, :]
                            pv = pcol(f"pos_{'kv'[kv]}{l}", 0, 16)
                            pv = bass.AP(pv.tensor, pv.offset, [pv.ap[0], [1, 16], [0, NCMP]])
                            ins = V.tensor_tensor(d, src, pv, ALU.add)
                        ins.then_inc(cmp_full, 1)
                    if 0 <= i - 1 < len(jobs) and tiles[jobs[i - 1]][0] == "gate":
                        dve.wait_ge(fg_turned, l + 1)
                        z, za, ze = z32[:, 0, :, :], z32[:, 1, :, :], z32[:, 2, :, :]
                        w_, s_, s2, p_, mz = (s8[:, n, :, :] for n in range(5))
                        zin = ps[4][:, 0:P].rearrange("p (t n) -> p t n", t=TT)
                        link(V.tensor_copy(z, zin))
                        link(V.tensor_copy(za, z))
                        V.scalar_tensor_tensor(out=za[:, :, 0:8], in0=z[:, :, 0:8], scalar=-1.0, in1=z[:, :, 0:8],
                                               op0=ALU.mult, op1=ALU.max).then_inc(fg_abs, 1)
                        link(V.tensor_scalar(mz, z[:, :, 0:8], 0.0, None, ALU.min))
                        dve.wait_ge(fg_exp, l + 1)
                        link(V.tensor_scalar(gates[:, :, :], ze[:, :, 8:32], 1.0, None, ALU.add))
                        link(V.reciprocal(gates[:, :, :], gates[:, :, :]))
                        e8 = ze[:, :, 0:8]
                        link(V.tensor_scalar(w_, e8, 2.0, None, ALU.add))
                        link(V.reciprocal(w_, w_))
                        link(V.tensor_tensor(s_, e8, w_, ALU.mult))
                        link(V.tensor_tensor(s2, s_, s_, ALU.mult))
                        link(V.tensor_scalar(p_, s2, 1.0 / 17, None, ALU.mult))
                        for k in (15, 13, 11, 9, 7, 5, 3):
                            link(V.scalar_tensor_tensor(out=p_, in0=p_, scalar=1.0 / k, in1=s2, op0=ALU.add, op1=ALU.mult))
                        link(V.scalar_tensor_tensor(out=p_, in0=p_, scalar=1.0, in1=s_, op0=ALU.add, op1=ALU.mult))
                        V.scalar_tensor_tensor(out=lf[:, :, :], in0=p_, scalar=-2.0, in1=mz, op0=ALU.mult,
                                               op1=ALU.add).then_inc(fg_log, 1)
                    if 0 <= i - 2 < len(jobs) and tiles[jobs[i - 2]][0] == "gate":
                        dve.wait_ge(fg_cum, l + 1)
                        cum = ps[4][0:8, :]
                        link(V.tensor_copy(c3[0:8, :], cum))
                        link(V.tensor_tensor(rt[0:8, :], cum, c3[0:8, :], ALU.subtract))
                        link(V.tensor_copy(mid_b[0:8, :], rt[0:8, :]))
                        V.tensor_copy(c3[32:40, :], mid_b[0:8, :])
                        link(V.tensor_tensor(t1[0:8, :], rt[0:8, :], mid_b[0:8, :], ALU.subtract))
                        V.tensor_copy(c3[64:72, :], t1[0:8, :]).then_inc(fg_parts, 1)
                    if 0 <= i - 2 < len(jobs) and tiles[jobs[i - 2]][0] in ("qr", "kr"):
                        t = jobs[i - 2]
                        kind, idx = tiles[t][:2]
                        a_ = tmp[:, roped_n % 2, :]
                        dve.wait_ge(rotated, roped_n + 1)
                        dve.wait_ge(fg_parts, l + 1)
                        dve.wait_ge(roped, roped_n)
                        link(V.tensor_tensor(t1[:, :], a_, cs2[:, 0, :], ALU.mult))
                        link(V.tensor_tensor(a_, ps[5][:, :], cs2[:, 1, :], ALU.mult))
                        if kind == "qr":
                            V.tensor_tensor(qb[:, idx, :], t1[:, :], a_, ALU.add).then_inc(roped, 1)
                        else:
                            V.tensor_tensor(ksw[0:64, idx, 0, :], t1[0:64, :], tmp[0:64, roped_n % 2, :], ALU.add)
                            V.tensor_tensor(ksw[64:128, idx, 1, :], t1[64:128, :], tmp[64:128, roped_n % 2, :],
                                            ALU.add).then_inc(roped, 1)
                        roped_n += 1
                dve.wait_ge(roped, roped_n)
                dve.wait_ge(cmp_out, 2 * l + 1)
                V.tensor_scalar(t1[:, 0:62], ps[4][:, 0:62], pcol(f"b2_k{l}"), None, ALU.add).then_inc(cmp_biased, 1)
                dve.wait_ge(cmp_out, 2 * l + 2)
                a_ = PAR[f"b2_v{l}"][0]
                link(V.tensor_tensor(tmp[0:NCMP, 2, 0:P], ps[6][0:NCMP, 0:P], par[0:NCMP, a_:a_ + P], ALU.add))
                for r in range(4):
                    ins = V.tensor_copy(vbd[32 * r:32 * r + NCMP, :, r * HD:(r + 1) * HD],
                                        tmp[0:NCMP, 2, 0:P].rearrange("p (g d) -> p g d", g=2))
                ins.then_inc(cmp_kept, 1)
                dve.wait_ge(cmp_rot, l + 1)
                for g in range(2):
                    cs_ = [cs2[:, n, CMP_LEN - 1:CMP_LEN - 1 + CMP_STEP * (NCMP - 1) + 1:CMP_STEP] for n in range(2)]
                    sl = slice(g * NCMP, (g + 1) * NCMP)
                    link(V.tensor_tensor(tmp[:, 0, sl], t1[:, sl], cs_[0], ALU.mult))
                    link(V.tensor_tensor(tmp[:, 1, sl], ps[5][:, sl], cs_[1], ALU.mult))
                    rows = slice(64 * g, 64 * g + 64)
                    ins = V.tensor_tensor(kc[rows, g, :], tmp[rows, 0, sl], tmp[rows, 1, sl], ALU.add)
                ins.then_inc(cmp_kept, 1)
                dve.wait_ge(cmp_kept, 2 * (l + 1))
                link(V.memset(cprob[:, :, NCMP:32], 0.0))
                u1 = FIRST["nsa", l] + len(UN)
                attend(FIRST["fox", l], u1, FIRST["nsa", l], ph["gates"])
                keep_turned(turned, [(ya_hi[:, c, :], ya_lo[:, c, :]) for c in range(4)]
                            + [(yn_hi[:, c, :], yn_lo[:, c, :]) for c in range(4)], [turn_bank(u1, c) for c in range(8)])
                turned += 8
                for m in range(DC):
                    fox_, nsa_ = ph["mix"][m]
                    if m == 1:
                        link(V.tensor_scalar(sg[:, 15, :], sg[:, 15, :], 1.0, None, ALU.add))
                        link(V.reciprocal(sg[:, 15, :], sg[:, 15, :]))
                    dve.wait_ge(blocks_done, filled(fox_))
                    if m:
                        dve.wait_ge(mix_full, DC * l + m)
                    V.tensor_tensor(mt[:, 0, :], ps[tiles[fox_][4]][:, :], sg[:, 2 * m, :], ALU.mult).then_inc(dve_took, 1)
                    V.tensor_tensor(mt[:, 1, :], ps[tiles[nsa_][4]][:, :], sg[:, 2 * m + 1, :], ALU.mult).then_inc(dve_took, 1)
                    dve.wait_ge(*took(nsa_))
                    V.tensor_tensor(tmp[:, m % 3, :], mt[:, 0, :], mt[:, 1, :], ALU.add).then_inc(mix_full, 1)
                    dve.wait_ge(mix_rounded, DC * l + m + 1)
                    V.tensor_tensor(mx_lo[:, m, :], tmp[:, m % 3, :], mx_hi[:, m, :].bitcast(f32),
                                    ALU.subtract).then_inc(mix_split, 1)
                add_residual(ph["out"], 4 + 2 * l)
                norm(4 + 2 * l, x, hn_hi, hn_lo)
                for half in range(2):
                    for i, t in enumerate(ph[f"up{half}"]):
                        n = 22 + 32 * l + 16 * half + i
                        dve.wait_ge(*took(t))
                        dve.wait_ge(ff_lo, n)
                        link(V.tensor_tensor(t1[:, :], tmp[:, n % 3, :], tmp[:, n % 3, :], ALU.mult))
                        dve.wait_ge(ff_hi, n + 1)
                        V.tensor_tensor(hid_lo[:, i, :], t1[:, :], hid_hi[:, i, :].bitcast(f32),
                                        ALU.subtract).then_inc(ff_lo, 1)
                    add_residual(ph[f"down{half}"], 5 + 2 * l if half else None)
            norm(7, x, None, None)


def _blocks(w, chunks=8):
    k, m = w.shape
    kc_, mt_ = k // P, m // P
    w = w.reshape(kc_, P, mt_, P).transpose(2, 1, 0, 3)
    pad = -kc_ % 8
    if pad:
        w = np.concatenate([w, np.zeros((mt_, P, pad, P), w.dtype)], axis=2)
    return w.reshape(mt_, P, (kc_ + pad) // 8, 1024).transpose(0, 2, 1, 3).reshape(-1, P, 1024)


def _stream(i):
    w, kvm = i["w_in"][0], i["w_mem_kv"][0]
    glu = w[:, 1536:2048].reshape(D, 2, 2, P).transpose(0, 2, 1, 3).reshape(D, 512)
    out = [_blocks(a) for a in (glu, w[:, :1024], w[:, 2048:], kvm[:, :256], w[:, 1024:1536], kvm[:, 256:],
                                i["w_out"][0])]
    up = i["w_up"][0].reshape(D, 2, 22, P).transpose(0, 2, 1, 3).reshape(D, 2 * FF1)
    out += [_blocks(up), _blocks(i["w_down"][0])]
    for l in range(LAYERS):
        w = i["w_in_2"][l]
        cut = np.cumsum([512, 512, 512, 8, 512, 768, 24, D])
        q_a, k_a, v_a, f_a, q_b, kv_b, g_b, ga, gb = np.split(w, cut, axis=1)
        fg = np.concatenate([f_a, g_b, np.zeros((D, P - 32), w.dtype)], axis=1)
        q_b = q_b.reshape(D, 2, 4, HD).transpose(0, 2, 1, 3).reshape(D, 512)
        kv = kv_b.reshape(D, 6, P)
        out += [_blocks(a) for a in (kv[:, 0], kv[:, 1], fg, k_a)]
        w1 = [_blocks(a) for a in i["cmp_w1_2"][l]]
        w1 = [w1[0][:2], w1[0][2:], w1[1][:2], w1[1][2:]]
        tail = np.concatenate([kv[:, n] for n in (2, 4, 3, 5)], axis=1)
        for n, a in enumerate((q_a, v_a, q_b, tail)):
            out += [w1[n], _blocks(a)]
        out.append(np.stack([_blocks(ga), _blocks(gb)], axis=1).reshape(-1, P, 1024))
        out.append(_blocks(np.concatenate([i["w_o_fox_2"][l], i["w_o_nsa_2"][l]], axis=0)))
        out.append(_blocks(i["w_out_2"][l]))
        for half in range(2):
            a, b = half * 2048, (half + 1) * 2048
            out += [_blocks(i["w_up_2"][l][:, a:b]), _blocks(i["w_down_2"][l][a:b])]
    return np.ascontiguousarray(np.concatenate(out, axis=0))


def _params(i):
    f = np.float32
    par = np.zeros((P, NPAR), f)

    def put(name, a):
        at, w = PAR[name]
        par[:a.shape[0], at:at + w] = a

    def chunks(v):
        return v.reshape(-1, P).T
    put("mix_g", chunks(i["mix_norm_g"][0]))
    put("mem_g", chunks(i["mem_norm_g"][0]))
    put("ffn_g", chunks(i["ffn_norm_g"][0]))
    for name, key in (("q_g", "q_norm_g"), ("k_g", "k_norm_g"), ("mq_g", "mq_norm_g"), ("mk_g", "mk_norm_g")):
        put(name, np.concatenate([i[key][0]] * 2)[:, None])
    put("conv_w", i["conv_dw_w"][0].reshape(CONV_K, 2, P).transpose(2, 1, 0).reshape(P, -1))
    put("conv_b", chunks(i["conv_dw_b"][0]))
    put("ln_g", chunks(i["conv_ln_g"][0]))
    put("ln_b", chunks(i["conv_ln_b"][0]))
    put("ffn_w", i["ffn_dw_w"][0].reshape(3, 44, P).transpose(2, 1, 0).reshape(P, -1))
    put("ffn_b", chunks(i["ffn_dw_b"][0]))
    put("eps", np.full((P, 1), EPS, f))
    put("eps64", np.full((P, 1), 64 * EPS, f))
    put("norm_final", chunks(i["norm_final_2"]))
    inv = _inv_freq()
    a = np.zeros((P, 1), f)
    for h in (0, 64):
        a[h:h + 8, 0] = a[h + 8:h + 16, 0] = inv
    put("inv_freq", a)
    for l in range(LAYERS):
        put(f"norm_mix{l}", chunks(i["norm_mix_2"][l]))
        put(f"norm_mlp{l}", chunks(i["norm_mlp_2"][l]))
        put(f"fgate_b{l}", i["b_forget_2"][l][:, None])
        for n, kv in enumerate("kv"):
            put(f"pos_{kv}{l}", i["cmp_pos_2"][l][n].reshape(16, P).T)
            put(f"b1_{kv}{l}", chunks(i["cmp_b1_2"][l][n]))
        put(f"b2_k{l}", np.concatenate([i["cmp_b2_2"][l][0]] * 2)[:, None])
        put(f"b2_v{l}", np.broadcast_to(np.concatenate([i["cmp_b2_2"][l][1]] * 2), (P, P)))
        w2 = i["cmp_w2_2"][l].reshape(2, 2, P, HD)
        put(f"w2_k{l}", np.concatenate([w2[0], w2[0]], axis=2).transpose(1, 0, 2).reshape(P, -1))
        put(f"w2_v{l}", w2[1].transpose(1, 0, 2).reshape(P, -1))
    return par


def _inv_freq():
    f = np.float32
    return np.power(f(500000.0), -np.arange(0, 16, 2, dtype=f) / f(16)).astype(f)


def _constants():
    f = np.float32
    p = np.arange(P)
    rot = np.zeros((P, P), f)
    for h in (0, 64):
        for d in range(8):
            rot[h + d + 8, h + d] = -1.0
            rot[h + d, h + d + 8] = 1.0
    headmean = (p[:, None] // HD == p[None, :] // HD).astype(f) / HD
    tri = (np.arange(S)[None, :] >= p[:, None]).astype(f)
    end = np.arange(NCMP) * CMP_STEP + CMP_LEN - 1
    valid0 = np.zeros((P, 32), f)
    valid0[:, :NCMP] = end[None, :] <= p[:, None]
    fconst = np.concatenate([np.eye(P, dtype=f), rot, headmean, np.full((P, P), 1 / D, f),
                             np.full((P, P), 1 / CONV_W, f), tri, valid0], axis=1)
    causal = np.where(p[None, :] > p[:, None], f(BIG), f(0))
    q = np.arange(S).reshape(TT, P).T
    cmask = np.where(end[None, None, None, :] <= q[:, :, None, None], f(0), f(BIG))
    cmask = np.broadcast_to(cmask, (P, TT, 8, NCMP)).reshape(P, -1)
    sel = np.zeros((P, 8, P), f)
    for h in range(8):
        for part in (0, 32, 64):
            sel[part + h, h, :] = 1.0
    bconst = np.concatenate([np.eye(P, dtype=f), causal, cmask, sel.reshape(P, -1)], axis=1).astype(np.dtype("bfloat16"))
    i = np.arange(S)
    gap = np.abs(i[:, None] - i[None, :])
    count = (gap <= 64).astype(int) + ((gap % 4 == 0) & (gap <= 256)) + ((gap % 16 == 0) & (gap <= 1024))
    lnc = np.where(count > 0, -np.log(np.maximum(count, 1)), BIG).astype(f)
    lnc = lnc.reshape(TT, P, S).transpose(1, 0, 2)
    inv = np.zeros((P, 1), f)
    for h in (0, 64):
        inv[h:h + 8, 0] = inv[h + 8:h + 16, 0] = _inv_freq()
    ang = (i[None, :].astype(f) * inv).astype(f)
    trig2 = np.stack([np.cos(ang), np.sin(ang)], axis=1).astype(f)
    return fconst, bconst, np.ascontiguousarray(lnc), np.ascontiguousarray(trig2)


def kernel(**inputs):
    import concourse.bacc as bacc
    from concourse.bass_utils import run_bass_kernel_spmd

    i = {k: np.asarray(v) for k, v in inputs.items()}
    fconst, bconst, lnc, trig2 = _constants()
    arrays = {
        "xT": np.ascontiguousarray(i["x"][0].T.reshape(DC, P, S).transpose(1, 0, 2)),
        "memT": np.ascontiguousarray(i["mem"][0].T.reshape(DC, P, NMEM).transpose(1, 0, 2)),
        "positions": np.ascontiguousarray(i["positions"]),
        "wstream": _stream(i), "params": _params(i), "fconst": fconst, "bconst": bconst,
        "lncount": lnc, "trig2": trig2,
    }
    nc = bacc.Bacc("TRN2", target_bir_lowering=False, num_devices=1)
    aps = [nc.dram_tensor(n, a.shape, mybir.dt.from_np(a.dtype), kind="ExternalInput").ap() for n, a in arrays.items()]
    out = nc.dram_tensor("out", (P, DC, S), mybir.dt.float32, kind="ExternalOutput").ap()
    build(nc, *aps, out)
    got = run_bass_kernel_spmd(nc, [arrays], core_ids=[0]).results[0]["out"]
    return np.ascontiguousarray(got.transpose(1, 0, 2).reshape(D, S).T)[None]
```
